# Optimizing a Trainium2 kernel written in Bass

```python
import jax
import jax.numpy as jnp
from jax import lax
import numpy as np

D_MODEL = 1024
BATCH = 1
SEQ = 1024
DEPTH = 2
DEC_BATCH = 8
DEC_SEQ = 4
PAST_LEN = 4096
PAGE_SIZE = 128

D_HEAD = 64
H_SB = 8
H_DSA = 8
KV_DSA = 2
H_IDX = 8
D_IDX = 64
DSA_TOPK = 256
Q_BLOCK = 128
ROPE_THETA = 10000.0
RK_N = 64
RK_H = D_MODEL // RK_N
RK_DECAY_LORA = 64
RK_AAA_LORA = 64
RK_GATE_LORA = 160
RK_GN_EPS = 64e-5
D_FF = 2816
CONV_W = 3
NORM_EPS = 1e-6
N_ATT_LAYERS = (DEPTH + 1) // 2
N_RWKV_LAYERS = DEPTH // 2
ATT_WIDTH = (H_SB + H_DSA) * D_HEAD
SPLIT_SIZES = (H_SB * D_HEAD, H_SB * D_HEAD, H_SB * D_HEAD,
               H_DSA * D_HEAD, KV_DSA * D_HEAD, KV_DSA * D_HEAD,
               H_IDX * D_IDX, D_IDX, H_IDX)
SPLIT_POINTS = [int(s) for s in np.cumsum(SPLIT_SIZES)[:-1]]
ATT_IN = int(sum(SPLIT_SIZES))

kernel_name = 'sb_dsa_rwkv7_convffn_step'

def rms_norm(x, g):
    xf = x.astype(jnp.float32)
    y = xf * lax.rsqrt(jnp.mean(xf * xf, axis=-1, keepdims=True) + NORM_EPS)
    return (y * g.astype(jnp.float32)).astype(x.dtype)

def rope(x, pos):
    half = x.shape[-1] // 2
    inv = ROPE_THETA ** (-2.0 * jnp.arange(half, dtype=jnp.float32) / x.shape[-1])
    ang = pos.astype(jnp.float32)[:, None] * inv[None, :]
    cos = jnp.cos(ang)[None, :, None, :]
    sin = jnp.sin(ang)[None, :, None, :]
    xf = x.astype(jnp.float32)
    x1, x2 = xf[..., :half], xf[..., half:]
    return jnp.concatenate([x1 * cos - x2 * sin, x2 * cos + x1 * sin], axis=-1).astype(x.dtype)

def gather_pages(cache, layer, page_table):
    g = cache[layer, page_table]
    return g.reshape((g.shape[0], g.shape[1] * g.shape[2]) + g.shape[3:])

def stick_breaking(q, k, v, q_pos, k_pos):
    z = jnp.einsum('bqhd,blhd->bhql', q, k).astype(jnp.float32) * (D_HEAD ** -0.5)
    mask = (k_pos[None, :] < q_pos[:, None])[None, None]
    log_beta = jax.nn.log_sigmoid(z)
    log_keep = jnp.where(mask, log_beta - z, 0.0)
    after = lax.cumsum(log_keep, axis=3, reverse=True) - log_keep
    w = jnp.where(mask, jnp.exp(log_beta + after), 0.0)
    return jnp.einsum('bhql,blhd->bqhd', w.astype(v.dtype), v)

def dsa_attention(q, k, v, q_idx, k_idx, w_idx, q_pos, k_pos, n_sel):
    B, Q = q.shape[0], q.shape[1]
    s = jnp.einsum('bqhd,bld->bqhl', q_idx, k_idx).astype(jnp.float32)
    score = jnp.einsum('bqh,bqhl->bql', w_idx.astype(jnp.float32), jax.nn.relu(s)) * (D_IDX ** -0.5 * H_IDX ** -0.5)
    causal = (k_pos[None, :] <= q_pos[:, None])[None]
    score = jnp.where(causal, score, -jnp.inf)
    _, sel = lax.top_k(score, n_sel)
    valid = sel <= q_pos[None, :, None]
    take = jax.vmap(lambda a, i: a[i])
    kg = take(k, sel)
    vg = take(v, sel)
    qg = q.reshape(B, Q, KV_DSA, H_DSA // KV_DSA, D_HEAD)
    logits = jnp.einsum('bqgrd,bqkgd->bqgrk', qg, kg).astype(jnp.float32) * (D_HEAD ** -0.5)
    logits = jnp.where(valid[:, :, None, None, :], logits, -jnp.inf)
    p = jax.nn.softmax(logits, axis=-1)
    o = jnp.einsum('bqgrk,bqkgd->bqgrd', p.astype(v.dtype), vg)
    return o.reshape(B, Q, H_DSA, D_HEAD)

def attn_mixer(h, w_in, w_out, past):
    Bt, T, _ = h.shape
    P = 0 if past is None else past[0].shape[1]
    L = P + T
    pos = P + jnp.arange(T, dtype=jnp.int32)
    proj = h @ w_in
    qa, ka, va, qb, kb, vb, qi, ki, wi = jnp.split(proj, SPLIT_POINTS, axis=-1)
    qa = qa.reshape(Bt, T, H_SB, D_HEAD)
    ka = ka.reshape(Bt, T, H_SB, D_HEAD)
    va = va.reshape(Bt, T, H_SB, D_HEAD)
    qb = rope(qb.reshape(Bt, T, H_DSA, D_HEAD), pos)
    kb = rope(kb.reshape(Bt, T, KV_DSA, D_HEAD), pos)
    vb = vb.reshape(Bt, T, KV_DSA, D_HEAD)
    qi = rope(qi.reshape(Bt, T, H_IDX, D_IDX), pos)
    ki = rope(ki[:, :, None, :], pos)[:, :, 0, :]
    new_rows = (ka, va, kb, vb, ki)
    if past is None:
        KA, VA, KB, VB, KI = new_rows
    else:
        KA, VA, KB, VB, KI = (jnp.concatenate([p_.astype(n_.dtype), n_], axis=1) for p_, n_ in zip(past, new_rows))
    k_pos = jnp.arange(L, dtype=jnp.int32)
    qb_len = min(Q_BLOCK, T)
    n_blocks = T // qb_len
    n_sel = min(DSA_TOPK, L // 4)

    def block(i):
        start = i * qb_len
        sl = lambda a: lax.dynamic_slice_in_dim(a, start, qb_len, axis=1)
        qp = lax.dynamic_slice_in_dim(pos, start, qb_len)
        oa = stick_breaking(sl(qa), KA, VA, qp, k_pos)
        ob = dsa_attention(sl(qb), KB, VB, sl(qi), KI, sl(wi), qp, k_pos, n_sel)
        return jnp.concatenate([oa.reshape(Bt, qb_len, H_SB * D_HEAD), ob.reshape(Bt, qb_len, H_DSA * D_HEAD)], axis=-1)

    o = lax.map(block, jnp.arange(n_blocks))
    o = jnp.transpose(o, (1, 0, 2, 3)).reshape(Bt, T, ATT_WIDTH)
    return o @ w_out, new_rows

def rwkv7_mixer(h, shift_prev, S0, mix, w_r, w_k, w_v, w_o, w0, w1, w2, a0, a1, a2, g1, g2, k_k, k_a, r_k, ln_w, ln_b):
    Bt, T, D = h.shape
    x_prev = jnp.concatenate([shift_prev[:, None, :].astype(h.dtype), h[:, :-1]], axis=1)
    xx = x_prev - h
    xr, xw, xk, xv, xa, xg = (h + xx * mix[j] for j in range(6))
    r = xr @ w_r
    k = xk @ w_k
    v = xv @ w_v
    w_log = -jax.nn.softplus(-(w0 + jnp.tanh(xw @ w1) @ w2).astype(jnp.float32)) - 0.5
    a = jax.nn.sigmoid((a0 + (xa @ a1) @ a2).astype(jnp.float32))
    g = jax.nn.sigmoid(xg @ g1) @ g2
    hs = lambda t: t.reshape(Bt, T, RK_H, RK_N)
    kk = hs((k * k_k).astype(jnp.float32))
    kk = kk / jnp.maximum(jnp.sqrt(jnp.sum(kk * kk, axis=-1, keepdims=True)), 1e-12)
    kf = k.astype(jnp.float32) * (1.0 + (a - 1.0) * k_a.astype(jnp.float32))
    decay = jnp.exp(-jnp.exp(w_log))
    rf = hs(r.astype(jnp.float32))
    kh = hs(kf)
    vf = hs(v.astype(jnp.float32))
    seqs = (rf, hs(decay), kh, vf, -kk, kk * hs(a))
    seqs = tuple(jnp.moveaxis(t, 1, 0) for t in seqs)

    def step(S, inp):
        r_t, d_t, k_t, v_t, av_t, bv_t = inp
        sa = jnp.einsum('bhij,bhj->bhi', S, av_t)
        S = S * d_t[:, :, None, :] + sa[..., None] * bv_t[:, :, None, :] + v_t[..., None] * k_t[:, :, None, :]
        return S, jnp.einsum('bhij,bhj->bhi', S, r_t)

    S_fin, y = lax.scan(step, S0.astype(jnp.float32), seqs)
    y = jnp.moveaxis(y, 0, 1)
    mu = jnp.mean(y, axis=-1, keepdims=True)
    var = jnp.mean(jnp.square(y - mu), axis=-1, keepdims=True)
    yn = ((y - mu) * lax.rsqrt(var + RK_GN_EPS)).reshape(Bt, T, D) * ln_w.astype(jnp.float32) + ln_b.astype(jnp.float32)
    bonus = jnp.sum(rf * kh * r_k.astype(jnp.float32), axis=-1, keepdims=True) * vf
    out = ((yn + bonus.reshape(Bt, T, D)) * g.astype(jnp.float32)).astype(h.dtype) @ w_o
    return out, h[:, -1], S_fin.astype(h.dtype)

def conv_ffn(h, w_up, conv_w, conv_b, w_down, prev):
    T = h.shape[1]
    u = h @ w_up
    full = jnp.concatenate([prev.astype(u.dtype), u], axis=1)
    c = conv_b + sum(conv_w[j] * full[:, j:j + T] for j in range(CONV_W))
    gate, val = jnp.split(c, 2, axis=-1)
    y = (jax.nn.gelu(gate, approximate=True) * val) @ w_down
    return y, full[:, full.shape[1] - (CONV_W - 1):]

def setup_inputs(seed: int = 0) -> dict:
    key = jax.random.key(seed)
    keys = jax.random.split(key, 64)
    counter = [0]

    def nk():
        kk_ = keys[counter[0]]
        counter[0] += 1
        return kk_

    def nrm(shape, scale):
        return jax.random.normal(nk(), shape, jnp.float32) * scale

    n_pages = PAST_LEN // PAGE_SIZE
    n_used = DEC_BATCH * n_pages
    n_pool = n_used + n_used // 4
    NA, NR, D = N_ATT_LAYERS, N_RWKV_LAYERS, D_MODEL
    inp = {}
    inp['x_prompt'] = nrm((BATCH, SEQ, D), 1.0)
    inp['x_sample'] = nrm((DEC_BATCH, DEC_SEQ, D), 1.0)
    inp['cache_sb_k'] = nrm((NA, n_pool, PAGE_SIZE, H_SB, D_HEAD), 1.0)
    inp['cache_sb_v'] = nrm((NA, n_pool, PAGE_SIZE, H_SB, D_HEAD), 1.0)
    inp['cache_dsa_k'] = nrm((NA, n_pool, PAGE_SIZE, KV_DSA, D_HEAD), 1.0)
    inp['cache_dsa_v'] = nrm((NA, n_pool, PAGE_SIZE, KV_DSA, D_HEAD), 1.0)
    inp['cache_idx_k'] = nrm((NA, n_pool, PAGE_SIZE, D_IDX), 1.0)
    inp['page_table'] = jax.random.permutation(nk(), n_pool)[:n_used].reshape(DEC_BATCH, n_pages).astype(jnp.int32)
    inp['state_wkv'] = nrm((NR, DEC_BATCH, RK_H, RK_N, RK_N), 0.3)
    inp['state_shift'] = nrm((NR, DEC_BATCH, D), 1.0)
    inp['state_ffn_conv'] = nrm((DEPTH, DEC_BATCH, CONV_W - 1, 2 * D_FF), 1.0)
    inp['norm_mix_pre'] = 1.0 + nrm((DEPTH, D), 0.05)
    inp['norm_mix_post'] = 1.0 + nrm((DEPTH, D), 0.05)
    inp['norm_ffn_pre'] = 1.0 + nrm((DEPTH, D), 0.05)
    inp['norm_ffn_post'] = 1.0 + nrm((DEPTH, D), 0.05)
    inp['att_w_in'] = nrm((NA, D, ATT_IN), D ** -0.5)
    inp['att_w_out'] = nrm((NA, ATT_WIDTH, D), ATT_WIDTH ** -0.5)
    inp['rk_mix'] = jax.random.uniform(nk(), (NR, 6, D), jnp.float32)
    inp['rk_w_r'] = nrm((NR, D, D), D ** -0.5)
    inp['rk_w_k'] = nrm((NR, D, D), D ** -0.5)
    inp['rk_w_v'] = nrm((NR, D, D), D ** -0.5)
    inp['rk_w_o'] = nrm((NR, D, D), D ** -0.5)
    inp['rk_w0'] = jax.random.uniform(nk(), (NR, D), jnp.float32, minval=-6.0, maxval=1.0)
    inp['rk_w1'] = nrm((NR, D, RK_DECAY_LORA), D ** -0.5)
    inp['rk_w2'] = nrm((NR, RK_DECAY_LORA, D), 0.5 * RK_DECAY_LORA ** -0.5)
    inp['rk_a0'] = nrm((NR, D), 0.1)
    inp['rk_a1'] = nrm((NR, D, RK_AAA_LORA), D ** -0.5)
    inp['rk_a2'] = nrm((NR, RK_AAA_LORA, D), 0.5 * RK_AAA_LORA ** -0.5)
    inp['rk_g1'] = nrm((NR, D, RK_GATE_LORA), D ** -0.5)
    inp['rk_g2'] = nrm((NR, RK_GATE_LORA, D), RK_GATE_LORA ** -0.5)
    inp['rk_k_k'] = 0.85 + nrm((NR, D), 0.05)
    inp['rk_k_a'] = 1.0 + nrm((NR, D), 0.05)
    inp['rk_r_k'] = nrm((NR, RK_H, RK_N), 0.1)
    inp['rk_ln_w'] = 1.0 + nrm((NR, D), 0.05)
    inp['rk_ln_b'] = nrm((NR, D), 0.01)
    inp['ffn_w_up'] = nrm((DEPTH, D, 2 * D_FF), D ** -0.5)
    inp['ffn_conv_w'] = nrm((DEPTH, CONV_W, 2 * D_FF), CONV_W ** -0.5)
    inp['ffn_conv_b'] = nrm((DEPTH, 2 * D_FF), 0.01)
    inp['ffn_w_down'] = nrm((DEPTH, D_FF, D), D_FF ** -0.5)
    return inp

def reference(x_prompt, x_sample, cache_sb_k, cache_sb_v, cache_dsa_k, cache_dsa_v, cache_idx_k, page_table,
              state_wkv, state_shift, state_ffn_conv,
              norm_mix_pre, norm_mix_post, norm_ffn_pre, norm_ffn_post,
              att_w_in, att_w_out,
              rk_mix, rk_w_r, rk_w_k, rk_w_v, rk_w_o, rk_w0, rk_w1, rk_w2, rk_a0, rk_a1, rk_a2,
              rk_g1, rk_g2, rk_k_k, rk_k_a, rk_r_k, rk_ln_w, rk_ln_b,
              ffn_w_up, ffn_conv_w, ffn_conv_b, ffn_w_down):
    xp, xs = x_prompt, x_sample
    Bp = xp.shape[0]
    att_p, att_s, wkv_p, wkv_s, sh_p, sh_s, cv_p, cv_s = [], [], [], [], [], [], [], []
    for i in range(DEPTH):
        li = i // 2
        hp = rms_norm(xp, norm_mix_pre[i])
        hs = rms_norm(xs, norm_mix_pre[i])
        if i % 2 == 0:
            past = tuple(gather_pages(c, li, page_table) for c in (cache_sb_k, cache_sb_v, cache_dsa_k, cache_dsa_v, cache_idx_k))
            op, rows_p = attn_mixer(hp, att_w_in[li], att_w_out[li], None)
            os_, rows_s = attn_mixer(hs, att_w_in[li], att_w_out[li], past)
            att_p.append(rows_p)
            att_s.append(rows_s)
        else:
            prm = (rk_mix[li], rk_w_r[li], rk_w_k[li], rk_w_v[li], rk_w_o[li], rk_w0[li], rk_w1[li], rk_w2[li],
                   rk_a0[li], rk_a1[li], rk_a2[li], rk_g1[li], rk_g2[li], rk_k_k[li], rk_k_a[li], rk_r_k[li],
                   rk_ln_w[li], rk_ln_b[li])
            zero_shift = jnp.zeros((Bp, D_MODEL), xp.dtype)
            zero_wkv = jnp.zeros((Bp, RK_H, RK_N, RK_N), jnp.float32)
            op, shp, Sp = rwkv7_mixer(hp, zero_shift, zero_wkv, *prm)
            os_, shs, Ss = rwkv7_mixer(hs, state_shift[li], state_wkv[li], *prm)
            wkv_p.append(Sp)
            wkv_s.append(Ss)
            sh_p.append(shp)
            sh_s.append(shs)
        xp = xp + rms_norm(op, norm_mix_post[i])
        xs = xs + rms_norm(os_, norm_mix_post[i])
        hp = rms_norm(xp, norm_ffn_pre[i])
        hs = rms_norm(xs, norm_ffn_pre[i])
        fp, cp = conv_ffn(hp, ffn_w_up[i], ffn_conv_w[i], ffn_conv_b[i], ffn_w_down[i],
                          jnp.zeros((Bp, CONV_W - 1, 2 * D_FF), xp.dtype))
        fs, cs = conv_ffn(hs, ffn_w_up[i], ffn_conv_w[i], ffn_conv_b[i], ffn_w_down[i], state_ffn_conv[i])
        cv_p.append(cp)
        cv_s.append(cs)
        xp = xp + rms_norm(fp, norm_ffn_post[i])
        xs = xs + rms_norm(fs, norm_ffn_post[i])
    st = lambda rows, j: jnp.stack([r[j] for r in rows])
    return (xp, xs,
            st(att_p, 0), st(att_s, 0), st(att_p, 1), st(att_s, 1),
            st(att_p, 2), st(att_s, 2), st(att_p, 3), st(att_s, 3),
            st(att_p, 4), st(att_s, 4),
            jnp.stack(wkv_p), jnp.stack(wkv_s), jnp.stack(sh_p), jnp.stack(sh_s),
            jnp.stack(cv_p), jnp.stack(cv_s))


_drawn_inputs = setup_inputs


def setup_inputs(seed=0):
    import zlib

    import numpy as np

    out = dict(_drawn_inputs(seed))
    spreads = {}
    factors = {'rk_ln_b': 8.0, 'ffn_conv_b': 4.141}
    for name, (base, spread) in spreads.items():
        noise = np.random.default_rng([zlib.crc32(name.encode()), seed]).standard_normal(out[name].shape)
        drawn = base * np.exp(spread * noise) if base else spread * noise
        out[name] = jnp.asarray(drawn.astype(out[name].dtype))
    for name, factor in factors.items():
        out[name] = (out[name] * factor).astype(out[name].dtype)
    return out
```

```python
from contextlib import ExitStack

import concourse.bass as bass
from concourse import mybir

F32 = mybir.dt.float32
BF16 = mybir.dt.bfloat16
I32 = mybir.dt.int32
ACT = mybir.ActivationFunctionType
ALU = mybir.AluOpType
AX = mybir.AxisListType

P = 128
D = 1024
KD = D // P
SEQ = 1024
NT = SEQ // P
NB, NQ = 8, 4
NS = NB * NQ
T = SEQ + NS
NCH = 3
CW = T // NCH
PAST = 4096
PAGE = 128
NPG = PAST // PAGE
DH = 64
HP = 4
D_FF = 2816
KF = D_FF // P
EPS = 1e-6
FILL = -1e30
OFF_KA, OFF_VA, OFF_QB, OFF_KB, OFF_VB, OFF_QI, OFF_KI, OFF_WI = 512, 1024, 1536, 2048, 2176, 2304, 2816, 2880


class Link:

    def __init__(self, eng, sem):
        self.eng, self.sem, self.base, self.n, self.start = eng, sem, 0, 0, 0

    def __call__(self, ins):
        ins.then_inc(self.sem, 1)
        self.n += 1
        self.eng.wait_ge(self.sem, self.base + self.n)

    def enter(self, i, per):
        self.start = self.base + self.n
        self.base, self.n = i * per + self.start, 0

    def leave(self, times, per):
        assert self.n == per, (self.n, per)
        self.base, self.n = self.start + times * per, 0


class Stage:

    def __init__(self, nc, name):
        self.nc, self.name, self.sems = nc, name, []

    def __enter__(self):
        self.ctx = ExitStack()
        return self

    def sb(self, name, shape, dt=F32):
        return self.ctx.enter_context(self.nc.sbuf_tensor(f"{self.name}_{name}", shape, dt))

    def ps(self, name, shape, dt=F32):
        return self.ctx.enter_context(self.nc.psum_tensor(f"{self.name}_{name}", shape, dt))

    def sem(self, name):
        s = self.nc.alloc_semaphore(f"{self.name}_{name}")
        self.sems.append(s)
        return s

    def block(self):
        return self.ctx.enter_context(self.nc.Block())

    def __exit__(self, *exc):
        self.ctx.close()
        if exc[0] is None:
            self.nc.clear_and_free_semaphores(self.sems)
            self.nc.all_engine_barrier()
        return False


def chunks(ps):
    return ps[:, :, 0:CW]


def row3(ap):
    return ap.rearrange("p (c n) -> p c n", c=NCH)


def stage_constants(nc, K):
    with Stage(nc, "const") as s:
        made = s.sem("made")
        loaded = s.sem("loaded")
        block = s.block()

        @block.gpsimd
        def _(pool):
            pool.memset(K.ones[:, :], 1.0).then_inc(made, 1)
            pool.memset(K.negones[:, :], -1.0).then_inc(made, 1)
            pool.memset(K.eps[:, :], EPS).then_inc(made, 1)
            pool.memset(K.one[:, :], 1.0).then_inc(made, 1)
            pool.memset(K.zeros16[:, :], 0.0).then_inc(made, 1)
            pool.wait_ge(made, 5)
            pool.affine_select(out=K.ident[:, :], in_=K.ones[:, :], compare_op=ALU.is_equal, fill=0.0, base=0,
                               pattern=[[1, P]], channel_multiplier=-1).then_inc(made, 1)
            pool.affine_select(out=K.tri[:, :], in_=K.negones[:, :], compare_op=ALU.is_ge, fill=0.0, base=0,
                               pattern=[[-1, P]], channel_multiplier=1).then_inc(made, 1)
            pool.affine_select(out=K.before[:, :], in_=K.ones[:, :], compare_op=ALU.is_gt, fill=0.0, base=0,
                               pattern=[[1, P]], channel_multiplier=-1).then_inc(made, 1)
            pool.memset(K.bound[:, :], 3e38).then_inc(made, 1)
            pool.wait_ge(made, 9)
            pool.affine_select(out=K.bound[:, :], in_=K.bound[:, :], compare_op=ALU.is_gt, fill=0.0, base=0,
                               pattern=[[1, P]], channel_multiplier=-1).then_inc(made, 1)
            pool.memset(K.causal[:, :], 0.0).then_inc(made, 1)
            pool.wait_ge(made, 11)
            pool.affine_select(out=K.causal[:, :], in_=K.causal[:, :], compare_op=ALU.is_ge, fill=FILL, base=0,
                               pattern=[[-1, P]], channel_multiplier=1).then_inc(made, 1)
            pool.wait_ge(made, 12)


def stage_load_x(nc, K, x_prompt, x_sample, xT):
    with Stage(nc, "load") as s:
        xin = s.sb("xin", [P, NT + 1, D])
        tp = [s.ps(f"tp{i}", [P, KD, P]) for i in range(2)]
        loaded, turned, copied, saved = s.sem("loaded"), s.sem("turned"), s.sem("copied"), s.sem("saved")
        block = s.block()

        @block.sync
        def _(sp):
            sp.dma_start(xin[:, 0:NT, :], x_prompt[0].rearrange("(t p) d -> p t d", p=P)).then_inc(loaded, 16)
            sp.dma_start(xin[0:NS, NT, :], x_sample.rearrange("b t d -> (b t) d")).then_inc(loaded, 16)
            sp.wait_ge(copied, NT + 1)
            sp.dma_start(K.x_save, xT[:, :, :]).then_inc(saved, 16)
            sp.wait_ge(saved, 16)

        @block.tensor
        def _(pe):
            pe.wait_ge(loaded, 32)
            for t in range(NT + 1):
                rows = P if t < NT else NS
                if t >= 2:
                    pe.wait_ge(copied, t - 1)
                for k in range(KD):
                    last = pe.transpose(tp[t % 2][:, k, 0:rows], xin[0:rows, t, k * P:(k + 1) * P], K.ident[0:rows, 0:rows])
                last.then_inc(turned, 1)

        @block.vector
        def _(dve):
            for t in range(NT + 1):
                rows = P if t < NT else NS
                dve.wait_ge(turned, t + 1)
                dve.tensor_copy(xT[:, :, t * P:t * P + rows], tp[t % 2][:, :, 0:rows]).then_inc(copied, 1)


def stage_norm(nc, K, name, src, gain, dst, residual=None, square=None):
    with Stage(nc, name) as s:
        gcol = s.sb("gcol", [P, KD])
        rstd = s.sb("rstd", [P, T])
        if square is None:
            square = dst if residual is None else s.sb("square", [P, KD, T])
        total = s.ps("total", [P, NCH, 512])
        loaded, squared, summed, rooted, inverted, scaled = (s.sem(x) for x in (
            "loaded", "squared", "summed", "rooted", "inverted", "scaled"))
        added = s.sem("added")
        block = s.block()

        @block.sync
        def _(sp):
            with nc.allow_non_contiguous_dma(reason="4 KiB of gains, one per partition"):
                sp.dma_start(gcol[:, :], gain.rearrange("(k p) -> p k", p=P)).then_inc(loaded, 16)

        @block.scalar
        def _(act):
            for k in range(KD):
                act.activation(square[:, k, :], src[:, k, :], ACT.Square).then_inc(squared, 1)
            act.wait_ge(summed, 1)
            act.activation(row3(rstd[:, :]), chunks(total), ACT.Sqrt, bias=K.eps[:, 0:1], scale=1.0 / D).then_inc(rooted, 1)

        @block.tensor
        def _(pe):
            for k in range(KD):
                pe.wait_ge(squared, k + 1)
                for c in range(NCH):
                    last = pe.matmul(total[:, c, 0:CW], K.ones[:, :], square[:, k, c * CW:(c + 1) * CW],
                                     start=(k == 0), stop=(k == KD - 1))
            last.then_inc(summed, 1)

        @block.vector
        def _(dve):
            dve.wait_ge(loaded, 16)
            dve.wait_ge(rooted, 1)
            dve.reciprocal(rstd[:, :], rstd[:, :]).then_inc(inverted, 1)
            dve.wait_ge(inverted, 1)
            out = dst if residual is None else src
            for k in range(KD):
                dve.scalar_tensor_tensor(out=out[:, k, :], in0=src[:, k, :], scalar=gcol[:, k:k + 1], in1=rstd[:, :],
                                         op0=ALU.mult, op1=ALU.mult).then_inc(scaled, 1)
            if residual is not None:
                for k in range(KD):
                    dve.wait_ge(scaled, k + 1)
                    dve.tensor_tensor(residual[:, k, :], residual[:, k, :], src[:, k, :], ALU.add).then_inc(added, 1)


def stage_project(nc, K, w_in, hT, A, free):
    W = w_in[0].rearrange("(k p) n -> p k n", p=P)
    with Stage(nc, "proj") as s:
        w = [s.sb(f"w{u}", [P, KD, P]) for u in range(2)]
        cos, sin, half = (free[:, i, :] for i in range(3))
        acc = [s.ps(f"acc{u}", [P, NCH, 512]) for u in range(2)]
        w_loaded = [s.sem(f"w_loaded{u}") for u in range(2)]
        tables, product, taken, steps = s.sem("tables"), s.sem("product"), s.sem("taken"), s.sem("steps")
        block = s.block()
        DHS = bass.ds

        def pair_src(i, base):
            return [(W[:, :, DHS(i * P + base, P)], slice(0, P))]

        def qb_src(i):
            return [(W[:, :, DHS(i * DH + OFF_QB, DH)], slice(0, DH)),
                    (W[:, :, DHS(i * DH + OFF_QB + HP * DH, DH)], slice(DH, P))]

        ki = [(W[:, :, OFF_KI:OFF_KI + DH], slice(0, DH)), (W[:, :, OFF_KI:OFF_KI + DH], slice(DH, P))]
        wi = [(W[:, :, OFF_WI:OFF_WI + 8], slice(0, 8))]
        rounds = [
            (4, lambda i: pair_src(i, 0), "query", lambda i: A.qa[:, DHS(i, 1), :],
             lambda i: pair_src(i, OFF_KA), "copy", lambda i: A.ka[:, DHS(i, 1), :]),
            (4, lambda i: pair_src(i, OFF_VA), "copy", lambda i: A.va[:, DHS(i, 1), :],
             qb_src, "rope", lambda i: A.qb[:, DHS(i, 1), :]),
            (1, lambda i: pair_src(0, OFF_VB), "copy", lambda i: A.vb[:, :, :],
             lambda i: pair_src(0, OFF_KB), "rope", lambda i: A.kb[:, :, :]),
            (2, lambda i: pair_src(2 * i, OFF_QI), "rope", lambda i: A.qi[:, DHS(2 * i, 1), :],
             lambda i: pair_src(2 * i + 1, OFF_QI), "rope", lambda i: A.qi[:, DHS(2 * i + 1, 1), :]),
            (1, lambda i: ki, "rope", lambda i: A.ki[:, :, :],
             lambda i: wi, "weights", lambda i: A.wi[:, :]),
        ]
        n_loads = [[len(r[1 + 3 * u](0)) for u in range(2)] for r in rounds]

        @block.sync
        def _(sp):
            sp.dma_start(cos[:, :], K.cos).then_inc(tables, 16)
            sp.dma_start(sin[:, :], K.sin).then_inc(tables, 16)
            done = 0
            for n, r in enumerate(rounds):
                with sp.Fori(0, r[0]) as i:
                    for u in range(2):
                        if n > 0:
                            sp.wait_ge(product, 2 * i + 2 * done + u - 1)
                        else:
                            sp.wait_ge(product, 2 * i + u + 1)
                        for src, cols in r[1 + 3 * u](i):
                            sp.dma_start(w[u][:, :, cols], src).then_inc(w_loaded[u], 16)
                if n == 0:
                    done += r[0] + 1
                else:
                    done += r[0]

        @block.tensor
        def _(pe):
            pe.sem_inc(product, 2)
            done, loads = 0, [0, 0]
            for n, r in enumerate(rounds):
                with pe.Fori(0, r[0]) as i:
                    for u in range(2):
                        pe.wait_ge(w_loaded[u], 16 * (i * n_loads[n][u] + n_loads[n][u] + loads[u]))
                        pe.wait_ge(taken, 2 * i + 2 * done + u + 1)
                        m = 8 if r[2 + 3 * u] == "weights" else P
                        for c in range(NCH):
                            for k in range(KD):
                                last = pe.matmul(acc[u][0:m, c, 0:CW], w[u][:, k, 0:m], hT[:, k, c * CW:(c + 1) * CW],
                                                 start=(k == 0), stop=(k == KD - 1))
                        last.then_inc(product, 1)
                done += r[0]
                loads = [loads[u] + r[0] * n_loads[n][u] for u in range(2)]

        @block.vector
        def _(dve):
            dve.wait_ge(tables, 32)
            dve.sem_inc(taken, 2)
            link = Link(dve, steps)
            done = 0
            for n, r in enumerate(rounds):
                per = sum({"rope": 2}.get(r[2 + 3 * u], 0) for u in range(2))
                with dve.Fori(0, r[0]) as i:
                    if per:
                        link.enter(i, per)
                    for u in range(2):
                        kind, dst = r[2 + 3 * u], r[3 + 3 * u](i)
                        dve.wait_ge(product, 2 * i + 2 * done + u + 3)
                        if kind != "weights":
                            dst = dst.rearrange("p o (c n) -> p (o c) n", c=NCH)
                        if kind == "query":
                            dve.tensor_scalar(dst, chunks(acc[u]), DH ** -0.5, None, ALU.mult).then_inc(taken, 1)
                        elif kind == "copy":
                            dve.tensor_copy(dst, chunks(acc[u])).then_inc(taken, 1)
                        elif kind == "weights":
                            dve.tensor_copy(row3(dst), acc[u][0:8, :, 0:CW]).then_inc(taken, 1)
                        else:
                            dve.tensor_tensor(dst, chunks(acc[u]), row3(cos[:, :]), ALU.mult)
                            for q in range(4):
                                a, b = 32 * q, 32 * (q ^ 1)
                                last = dve.tensor_tensor(row3(half[a:a + 32, :]), acc[u][b:b + 32, :, 0:CW],
                                                         row3(sin[b:b + 32, :]), ALU.mult)
                            link(last)
                            link(dve.tensor_tensor(dst, dst, row3(half[:, :]), ALU.add))
                            dve.sem_inc(taken, 1)
                if per:
                    link.leave(r[0], per)
                done += r[0]


def stage_rows(nc, K, A, O):
    with Stage(nc, "rows") as s:
        row = [s.sb(f"row{i}", [P, 3, 512]) for i in range(2)]
        tp = [s.ps(f"tp{i}", [P, 3, 512]) for i in range(2)]
        turned, taken, stored, stepped = s.sem("turned"), s.sem("taken"), [s.sem(f"stored{i}") for i in range(2)], s.sem("stepped")
        block = s.block()

        @block.tensor
        def _(pe):
            for t in range(NT + 1):
                n = P if t < NT else NS
                cols = slice(t * P, t * P + n)
                if t >= 2:
                    pe.wait_ge(taken, 3 * (t - 1))
                for f in range(HP):
                    pe.transpose(tp[t % 2][0:n, 0, f * P:(f + 1) * P], A.ka[:, f, cols], K.ident[:, :])
                for f in range(HP):
                    pe.transpose(tp[t % 2][0:n, 1, f * P:(f + 1) * P], A.va[:, f, cols], K.ident[:, :])
                pe.transpose(tp[t % 2][0:n, 2, 0:P], A.kb[:, 0, cols], K.ident[:, :])
                pe.transpose(tp[t % 2][0:n, 2, P:2 * P], A.vb[:, 0, cols], K.ident[:, :])
                pe.transpose(tp[t % 2][0:n, 2, 2 * P:2 * P + DH], A.ki[0:DH, 0, cols], K.ident[0:DH, 0:DH])
                pe.transpose(tp[t % 2][0:n, 2, 320:328], A.wi[:, cols], K.ident[0:8, 0:8]).then_inc(turned, 1)

        @block.vector
        def _(dve):
            for t in range(NT + 1):
                n = P if t < NT else NS
                dve.wait_ge(turned, t + 1)
                if t >= 2:
                    dve.wait_ge(stored[t % 2], 80 * (t // 2))
                dve.tensor_copy(row[t % 2][0:n, 0, :], tp[t % 2][0:n, 0, :]).then_inc(taken, 1)
                dve.tensor_copy(row[t % 2][0:n, 1, :], tp[t % 2][0:n, 1, :]).then_inc(taken, 1)
                dve.tensor_copy(row[t % 2][0:n, 2, 0:328], tp[t % 2][0:n, 2, 0:328]).then_inc(taken, 1)
                dve.wait_ge(taken, 3 * t + 3)
                if t < NT:
                    dve.tensor_copy(A.vtok[:, t, 0:512], row[t % 2][:, 1, :])
                    dve.tensor_copy(A.vtok[:, t, 512:640], row[t % 2][:, 2, P:2 * P])
                dve.tensor_scalar(A.wtok[0:n, t, :], row[t % 2][0:n, 2, 320:328], (DH * 8) ** -0.5, None,
                                  ALU.mult).then_inc(stepped, 1)

        @block.sync
        def _(sp):
            for t in range(NT + 1):
                sp.wait_ge(taken, 3 * t + 3)
                r = row[t % 2]
                if t < NT:
                    n, rows = P, slice(t * P, (t + 1) * P)
                    dst = [o[0, 0][rows] for o in (O.sb_k_p, O.sb_v_p, O.dsa_k_p, O.dsa_v_p, O.idx_k_p)]
                    dst = [d.rearrange("t h d -> t (h d)") for d in dst[:4]] + dst[4:]
                else:
                    n = NS
                    dst = [o[0].rearrange("b t h d -> (b t) (h d)") for o in (O.sb_k_s, O.sb_v_s, O.dsa_k_s, O.dsa_v_s)]
                    dst.append(O.idx_k_s[0].rearrange("b t d -> (b t) d"))
                for d, src in zip(dst, (r[0:n, 0, :], r[0:n, 1, :], r[0:n, 2, 0:P], r[0:n, 2, P:2 * P], r[0:n, 2, 256:320])):
                    sp.dma_start(d, src).then_inc(stored[t % 2], 16)
            sp.wait_ge(stored[0], 80 * 5)
            sp.wait_ge(stored[1], 80 * 4)


def stage_stick_prompt(nc, K, A, oT):
    steps = [(qc, lt, par) for qc in range(2) for lt in range(qc * 4 + 3, -1, -1) for par in range(2)]
    n = len(steps)
    first = {qc: min(j for j in range(n) if steps[j][0] == qc) for qc in range(2)}
    diag = [j for j in range(n) if steps[j][1] >= steps[j][0] * 4]

    def col0(j):
        qc, lt, _ = steps[j]
        return max(lt - qc * 4, 0) * P

    B = 4
    with Stage(nc, "stick") as s:
        kst, qst = s.sb("kst", [P, SEQ]), s.sb("qst", [P, SEQ])
        capped, expd, sp_, wgt = (s.sb(x, [P, B, 512]) for x in ("capped", "expd", "softplus", "weight"))
        later = s.sb("later", [P, 2, B, 512])
        o_sb = s.sb("o_sb", [P, 512])
        z = [s.ps(f"z{i}", [P, 512]) for i in range(B)]
        o = [s.ps(f"o{i}", [P, 512]) for i in range(2)]
        oTp = s.ps("oTp", [P, 512])
        (staged, z_ready, capped_r, exp_r, ln_r, sp_ready, summed, w_ready, w_masked, w_used, o_copied,
         o_turned, o_taken, chain, added) = (s.sem(x) for x in (
             "staged", "z_ready", "capped", "exp", "ln", "sp_ready", "summed", "w_ready", "w_masked", "w_used",
             "o_copied", "o_turned", "o_taken", "chain", "added"))
        block = s.block()

        @block.gpsimd
        def _(pool):
            with pool.Fori(0, HP) as i:
                pool.wait_ge(w_used, n * i + B)
                pool.tensor_copy(kst[:, :], A.ka[:, bass.ds(i, 1), 0:SEQ].rearrange("p o n -> p (o n)")).then_inc(staged, 1)
                pool.tensor_copy(qst[:, :], A.qa[:, bass.ds(i, 1), 0:SEQ].rearrange("p o n -> p (o n)")).then_inc(staged, 1)

        @block.tensor
        def _(pe):
            pe.sem_inc(w_used, B)
            pe.sem_inc(o_turned, 1)
            with pe.Fori(0, HP) as i:
                pe.wait_ge(staged, 2 * i + 2)

                def scores(j):
                    qc, lt, par = steps[j]
                    c = col0(j)
                    pe.wait_ge(w_ready, n * i + j + 1)
                    h = slice(par * DH, par * DH + DH)
                    pe.matmul(z[j % B][:, c:512], kst[h, lt * P:(lt + 1) * P], qst[h, qc * 512 + c:qc * 512 + 512],
                              start=True, stop=False, skip_group_check=True).then_inc(z_ready, 1)

                def suffix(j):
                    qc, lt, par = steps[j]
                    c = col0(j)
                    pe.wait_ge(sp_ready, n * i + j + 1)
                    last = pe.matmul(z[j % B][:, c:512], K.tri[:, :], sp_[:, j % B, c:512], start=False, stop=True,
                                     skip_group_check=True)
                    if j - first[qc] >= 2:
                        last = pe.matmul(z[j % B][:, c:512], K.negones[:, :], later[:, par, (j // 2) % B, c:512],
                                         start=False, stop=True, skip_group_check=True)
                    last.then_inc(summed, 1)

                def output(j):
                    qc, lt, par = steps[j]
                    if j == first[qc]:
                        pe.wait_ge(o_copied, 2 * i + qc + 1)
                        pe.matmul(o[qc][:, :], K.zeros16[:, 0:P], K.zeros16[:, :], start=True, stop=False,
                                  skip_group_check=True)
                    if j in diag:
                        pe.wait_ge(w_masked, len(diag) * i + diag.index(j) + 1)
                    else:
                        pe.wait_ge(w_ready, n * i + j + 1 + B)
                    for q in range(col0(j) // P, 4):
                        last = pe.matmul(o[qc][:, q * P + par * DH:q * P + par * DH + DH], wgt[:, j % B, q * P:(q + 1) * P],
                                         A.vtok[:, lt, bass.ds(i * P + par * DH, DH)], start=False, stop=False,
                                         skip_group_check=True)
                    last.then_inc(w_used, 1)

                def turn(qc):
                    pe.wait_ge(o_copied, 2 * i + qc + 3)
                    pe.wait_ge(o_taken, 2 * i + qc + 1)
                    for q in range(4):
                        last = pe.transpose(oTp[:, q * P:(q + 1) * P], o_sb[:, q * P:(q + 1) * P], K.ident[:, :])
                    last.then_inc(o_turned, 1)

                for m in range(n + 3):
                    if m < n:
                        scores(m)
                    if 1 <= m < n + 1:
                        suffix(m - 1)
                    if m >= 3:
                        output(m - 3)
                        if m - 3 == first[1] + 3:
                            turn(0)
                turn(1)

        @block.scalar
        def _(act):
            act.preload_act_table_set("natural_log_exp_and_others")
            act.sem_inc(w_ready, B)
            act.sem_inc(o_taken, 1)
            with act.Fori(0, HP) as i:
                for m in range(n + 2):
                    if m < n:
                        c = col0(m)
                        act.wait_ge(capped_r, n * i + m + 1)
                        act.activation(expd[:, m % B, c:512], capped[:, m % B, c:512], ACT.Exp).then_inc(exp_r, 1)
                        act.wait_ge(exp_r, n * i + m + 1)
                        act.activation(expd[:, m % B, c:512], expd[:, m % B, c:512], ACT.Ln, bias=K.one[:, 0:1]).then_inc(ln_r, 1)
                    if m >= 2:
                        j = m - 2
                        c = col0(j)
                        act.wait_ge(summed, n * i + j + 1)
                        act.wait_ge(w_used, n * i + j + 1)
                        act.activation(wgt[:, j % B, c:512], z[j % B][:, c:512], ACT.Exp).then_inc(w_ready, 1)
                    if m in (first[1] + 6, n + 1):
                        qc = 0 if m < n else 1
                        act.wait_ge(o_turned, 2 * i + qc + 2)
                        act.activation(oT[:, bass.ds(i, 1), qc * 512:qc * 512 + 512].rearrange("p o n -> p (o n)"),
                                       oTp[:, :], ACT.Copy).then_inc(o_taken, 1)

        @block.vector
        def _(dve):
            dve.sem_inc(o_copied, 2)
            link = Link(dve, chain)
            sums = [j for j in range(n) if steps[j][1] > 0]
            with dve.Fori(0, HP) as i:
                link.enter(i, len(diag))
                for m in range(n + 3):
                    if m - 3 in diag:
                        j = m - 3
                        v = wgt[:, j % B, col0(j):col0(j) + P]
                        dve.wait_ge(w_ready, n * i + j + 1 + B)
                        dve.tensor_tensor(v, v, K.bound[:, :], ALU.min).then_inc(w_masked, 1)
                    if m < n:
                        dve.wait_ge(z_ready, n * i + m + 1)
                        dve.tensor_scalar(capped[:, m % B, col0(m):512], z[m % B][:, col0(m):512], 40.0, None,
                                          ALU.min).then_inc(capped_r, 1)
                    for qc, at in ((0, first[1] + 4), (1, n + 2)):
                        if m == at:
                            dve.wait_ge(w_used, n * i + B + (first[1] if qc == 0 else n))
                            dve.wait_ge(o_turned, 2 * i + qc + 1)
                            dve.tensor_copy(o_sb[:, :], o[qc][:, :]).then_inc(o_copied, 1)
                    if not 1 <= m <= n:
                        continue
                    j = m - 1
                    qc, lt, par = steps[j]
                    c = col0(j)
                    dve.wait_ge(ln_r, n * i + j + 1)
                    soft = sp_[:, j % B, c:512]
                    op = dve.tensor_tensor(soft, expd[:, j % B, c:512], z[j % B][:, c:512], ALU.max)
                    if j in diag:
                        link(op)
                        op = dve.tensor_tensor(sp_[:, j % B, c:c + P], sp_[:, j % B, c:c + P], K.before[:, :], ALU.mult)
                    op.then_inc(sp_ready, 1)
                    if j in sums:
                        k = j // 2
                        new = later[:, par, (k + 1) % B, :]
                        if c > 0:
                            dve.memset(new[:, c - P:c], 0.0)
                        dve.wait_ge(sp_ready, n * i + j + 1)
                        if j - first[qc] < 2:
                            dve.tensor_copy(new[:, c:512], soft).then_inc(added, 1)
                        else:
                            dve.wait_ge(added, len(sums) * i + sums.index(j - 2) + 1)
                            dve.tensor_tensor(new[:, c:512], soft, later[:, par, k % B, c:512], ALU.add).then_inc(added, 1)
                link.leave(HP, len(diag))


TOPK = 256
LOW = -3e38


def stage_sparse_prompt(nc, K, A, oT):
    units = []
    for qt in range(NT):
        if (qt + 1) * P > TOPK:
            units += [("index", qt, h) for h in range(8)]
        units += [("head", qt, h) for h in range(8)]
    heads = [u for u in units if u[0] == "head"]
    index = [u for u in units if u[0] == "index"]
    H, X = len(heads), len(index)
    with Stage(nc, "sparse") as s:
        score, bias = s.sb("score", [P, SEQ]), s.sb("bias", [P, SEQ])
        best = s.sb("best", [P, 8])
        kept, masked, prob, probT = ([s.sb(f"{x}{i}", [P, SEQ]) for i in range(2)] for x in ("kept", "masked", "prob", "probT"))
        top, negtop = ([s.sb(f"{x}{i}", [P, 1]) for i in range(4)] for x in ("top", "negtop"))
        total, inv = ([s.sb(f"{x}{i}", [P, 8]) for i in range(2)] for x in ("total", "inv"))
        o_sb = s.sb("o_sb", [P, 512])
        prod = [s.ps(f"prod{i}", [P, 1024]) for i in range(2)]
        turned_ps = s.ps("turned", [P, 1024])
        o = s.ps("o", [P, 512])
        oTp = s.ps("oTp", [P, 512])
        (product, relued, weighed, masked_r, negated, expd, p_turned, p_taken, o_ready, inverted, scaled, o_turned, o_taken,
         chain) = (s.sem(x) for x in ("product", "relued", "weighed", "masked", "negated", "expd", "p_turned", "p_taken",
                                      "o_ready", "inverted", "scaled", "o_turned", "o_taken", "chain"))
        block = s.block()

        def width(qt):
            return (qt + 1) * P

        def spans(qt):
            return [(a, min(a + 512, width(qt))) for a in range(0, width(qt), 512)]

        @block.tensor
        def _(pe):
            def multiply(u):
                kind, qt, h = units[u]
                if u >= 2:
                    before = units[u - 2]
                    if before[0] == "index":
                        pe.wait_ge(relued, index.index(before) + 1)
                    else:
                        pe.wait_ge(masked_r, heads.index(before) + 1)
                q, k = (A.qi, A.ki) if kind == "index" else (A.qb, A.kb)
                rows = slice((h % 2) * DH, (h % 2) * DH + DH)
                for a, b in spans(qt):
                    last = pe.matmul(prod[u % 2][:, a:b], q[rows, h // 2, qt * P:(qt + 1) * P], k[rows, 0, a:b],
                                     start=True, stop=True)
                last.then_inc(product, 1)

            def turn(j):
                _, qt, h = heads[j]
                pe.wait_ge(expd, j + 1)
                if j >= 1:
                    pe.wait_ge(p_taken, j)
                for l in range(qt + 1):
                    last = pe.transpose(turned_ps[:, l * P:(l + 1) * P], prob[j % 2][:, l * P:(l + 1) * P], K.ident[:, :])
                last.then_inc(p_turned, 1)

            def output(j):
                _, qt, h = heads[j]
                pe.wait_ge(p_taken, j + 1)
                if h == 0 and qt > 0:
                    pe.wait_ge(scaled, qt)
                for l in range(qt + 1):
                    last = pe.matmul(o[:, h * DH:(h + 1) * DH], probT[j % 2][:, l * P:(l + 1) * P],
                                     A.vtok[:, l, 512 + (h % 2) * DH:512 + (h % 2) * DH + DH], start=(l == 0), stop=(l == qt))
                last.then_inc(o_ready, 1)
                if h == 7:
                    pe.wait_ge(scaled, qt + 1)
                    if qt > 0:
                        pe.wait_ge(o_taken, qt)
                    for r in range(HP):
                        last = pe.transpose(oTp[:, r * P:(r + 1) * P], o_sb[:, r * P:(r + 1) * P], K.ident[:, :])
                    last.then_inc(o_turned, 1)

            pending = []
            for u in range(len(units)):
                multiply(u)
                if units[u][0] == "head":
                    j = heads.index(units[u])
                    if j >= 1:
                        turn(j - 1)
                    if j >= 2:
                        output(j - 2)
            turn(H - 1)
            output(H - 2)
            output(H - 1)

        @block.scalar
        def _(act):
            act.preload_act_table_set("natural_log_exp_and_others")

            def take(j):
                _, qt, h = heads[j]
                w = width(qt)
                act.wait_ge(p_turned, j + 1)
                if j >= 2:
                    act.wait_ge(o_ready, j - 1)
                act.activation(probT[j % 2][:, 0:w], turned_ps[:, 0:w], ACT.Copy).then_inc(p_taken, 1)

            def finish(qt):
                act.wait_ge(o_turned, qt + 1)
                act.activation(oT[:, HP:2 * HP, qt * P:(qt + 1) * P], oTp[:, :].rearrange("p (r q) -> p r q", r=HP),
                               ACT.Copy).then_inc(o_taken, 1)

            for u, unit in enumerate(units):
                kind, qt, h = unit
                w = width(qt)
                if kind == "index":
                    x = index.index(unit)
                    act.wait_ge(product, u + 1)
                    if x >= 2:
                        act.wait_ge(weighed, x - 1)
                    act.activation(kept[x % 2][:, 0:w], prod[u % 2][:, 0:w], ACT.Relu).then_inc(relued, 1)
                    continue
                j = heads.index(unit)
                act.wait_ge(negated, j + 1)
                if j >= 2:
                    act.wait_ge(p_turned, j - 1)
                act.activation(prob[j % 2][:, 0:w], masked[j % 2][:, 0:w], ACT.Exp, bias=negtop[j % 4][:, 0:1],
                               scale=DH ** -0.5, accum_out=total[qt % 2][:, h:h + 1]).then_inc(expd, 1)
                if j >= 1:
                    take(j - 1)
                if h == 2 and qt > 0:
                    finish(qt - 1)
            take(H - 1)
            finish(NT - 1)

        @block.vector
        def _(dve):
            link = Link(dve, chain)

            def normalise(qt):
                dve.wait_ge(expd, 8 * qt + 8)
                link(dve.reciprocal(inv[qt % 2][:, :], total[qt % 2][:, :]))
                dve.wait_ge(o_ready, 8 * qt + 8)
                if qt > 0:
                    dve.wait_ge(o_turned, qt)
                dve.tensor_tensor(o_sb[:, :].rearrange("p (h d) -> p h d", h=8), o[:, :].rearrange("p (h d) -> p h d", h=8),
                                  inv[qt % 2][:, :].unsqueeze(2).to_broadcast([P, 8, DH]), ALU.mult).then_inc(scaled, 1)

            for u, unit in enumerate(units):
                kind, qt, h = unit
                w = width(qt)
                if kind == "index":
                    x = index.index(unit)
                    dve.wait_ge(relued, x + 1)
                    if h == 0:
                        op = dve.tensor_scalar(score[:, 0:w], kept[x % 2][:, 0:w], A.wtok[:, qt, 0:1], None, ALU.mult)
                    else:
                        op = dve.scalar_tensor_tensor(out=score[:, 0:w], in0=kept[x % 2][:, 0:w], scalar=A.wtok[:, qt, h:h + 1],
                                                      in1=score[:, 0:w], op0=ALU.mult, op1=ALU.add)
                    op.then_inc(weighed, 1)
                    dve.wait_ge(weighed, x + 1)
                    if h == 7:
                        link(dve.tensor_tensor(score[:, w - P:w], score[:, w - P:w], K.causal[:, :], ALU.add))
                        for _ in range(TOPK // 8):
                            link(dve.max(best[:, :], score[:, 0:w]))
                            link(dve.match_replace(score[:, 0:w], best[:, :], score[:, 0:w], LOW))
                        link(dve.tensor_scalar(bias[:, 0:w], score[:, 0:w], LOW / 2, FILL, ALU.is_gt, ALU.mult))
                        link(dve.tensor_tensor(bias[:, w - P:w], bias[:, w - P:w], K.causal[:, :], ALU.add))
                    continue
                j = heads.index(unit)
                if h == 0 and width(qt) <= TOPK:
                    link(dve.memset(bias[:, 0:w], 0.0))
                    link(dve.tensor_tensor(bias[:, w - P:w], bias[:, w - P:w], K.causal[:, :], ALU.add))
                dve.wait_ge(product, u + 1)
                if j >= 2:
                    dve.wait_ge(expd, j - 1)
                dve.tensor_tensor_reduce(masked[j % 2][:, 0:w], prod[u % 2][:, 0:w], bias[:, 0:w], 1.0, FILL, ALU.add, ALU.max,
                                         top[j % 4][:, :]).then_inc(masked_r, 1)
                dve.wait_ge(masked_r, j + 1)
                dve.tensor_scalar(negtop[j % 4][:, :], top[j % 4][:, :], -(DH ** -0.5), None, ALU.mult).then_inc(negated, 1)
                if h == 1 and qt > 0:
                    normalise(qt - 1)
            normalise(NT - 1)


def page_numbers(nc, eng, pages, at, n, n_pool):
    _, values = nc.values_load_multi_w_load_instructions(
        pages[0:1, bass.ds(at, n)], engines=[eng.engine], min_val=0, max_val=n_pool - 1,
        skip_runtime_bounds_check_because="the load that the page number addresses has its own check against the cache's end")
    return values


def stage_stick_sample(nc, K, A, I, O, oT):
    NP1 = NPG + 1
    G = 8
    NG = NPG // G
    C = 32
    kc = I.cache_sb_k[0].rearrange("n p h d -> n p (h d)")
    vc = I.cache_sb_v[0].rearrange("n p h d -> n p (h d)")
    n_pool = kc.shape[0]
    with Stage(nc, "sstick") as s:
        pages = s.sb("pages", [1, NB * NPG], I32)
        kring, vring = s.sb("kring", [P, G, 512]), s.sb("vring", [P, G, 512])
        kT = s.sb("kT", [P, 2, 512])
        knew, vnew = s.sb("knew", [P, HP, P]), s.sb("vnew", [P, 512])
        q, qnow = s.sb("q", [P, HP, NB, 8]), s.sb("qnow", [P, HP, 8])
        new_q = s.sem("new_q")
        ok, bound = s.sb("ok", [P, C]), s.sb("bound", [P, C])
        soft, expd, later, wgt = (s.sb(x, [P, NP1 * C]) for x in ("soft", "expd", "later", "wgt"))
        z = s.ps("z", [P, 3 * 512])
        tp = [s.ps(f"tp{i}", [P, 512]) for i in range(2)]
        o, o2 = s.ps("o", [P, 512]), s.ps("o2", [P, 512])
        osb = s.sb("osb", [C, 512])
        best, score = s.sb("best", [NS, 8]), A.score[:, 0:PAST + NQ]
        o_copied, o_turned, passed, pe_passed = (s.sem(x) for x in ("o_copied", "o_turned", "passed", "pe_passed"))
        (table, made, qmade, v_used, turned, new_k, new_v, z_ready, capped, exp_r, ln_r, sp_ready, masked, later_r,
         summed, w_ready, w_masked, o_ready, o_taken, steps) = (s.sem(x) for x in (
             "table", "made", "qmade", "v_used", "turned", "new_k", "new_v", "z_ready", "capped", "exp", "ln",
             "sp_ready", "masked", "later", "summed", "w_ready", "w_masked", "o_ready", "o_taken", "steps"))
        scored = s.sem("scored")
        evac = [s.sem(f"evac{i}") for i in range(2)]
        k_in = [s.sem(f"k_in{i}") for i in range(G)]
        v_in = [s.sem(f"v_in{i}") for i in range(G)]
        block = s.block()
        banks = [(0, 512), (512, 1024), (1024, NP1 * C)]

        @block.sync
        def _(sp):
            sp.dma_start(pages[:, :], I.page_table.rearrange("(o b) n -> o (b n)", o=1)).then_inc(table, 16)
            sp.wait_ge(table, 16)

            def load(b, cache, ring, used, arrived):
                with sp.Fori(0, NG) as g:
                    numbers = page_numbers(nc, sp, pages, b * NPG + g * G, G, n_pool)
                    for u in range(G):
                        sp.wait_ge(used, b * NPG + g * G + u + 1)
                        sp.dma_start(ring[:, u, :], cache[bass.ds(numbers[u], 1)].rearrange("o p n -> p (o n)"))\
                            .then_inc(arrived[u], 16)

            def new_values(b):
                sp.wait_ge(o_taken, b + 1)
                sp.dma_start(vnew[0:NQ, :], O.sb_v_s[0][bass.ds(b, 1)].rearrange("o t h d -> (o t) (h d)")).then_inc(new_v, 16)

            load(0, kc, kring, turned, k_in)
            with sp.Fori(1, NB) as b:
                load(b, kc, kring, turned, k_in)
                load(b - 1, vc, vring, v_used, v_in)
                sp.wait_ge(made, 7)
                new_values(b - 1)
            load(NB - 1, vc, vring, v_used, v_in)
            new_values(NB - 1)

        @block.gpsimd
        def _(pool):
            pool.memset(knew[:, :, :], 0.0).then_inc(made, 1)
            pool.memset(vnew[:, :], 0.0).then_inc(made, 1)
            pool.memset(q[:, :, :, :], 0.0).then_inc(made, 1)
            pool.memset(ok[:, :], 1.0).then_inc(made, 1)
            pool.memset(bound[:, :], 3e38).then_inc(made, 1)
            pool.wait_ge(made, 5)
            for m in (ok, bound):
                v = m[:, :].rearrange("p (h q) -> p h q", q=NQ)
                pool.affine_select(out=v, in_=v, compare_op=ALU.is_gt, fill=0.0, base=0, pattern=[[0, 8], [1, NQ]],
                                   channel_multiplier=-1).then_inc(made, 1)
            with pool.Fori(0, NB) as b:
                pool.wait_ge(w_ready, b + 1)
                pool.wait_ge(qmade, 8)
                pool.tensor_copy(qnow[:, :, :], q[:, :, bass.ds(b, 1), :].rearrange("p f o n -> p f (o n)")).then_inc(new_q, 1)
                pool.tensor_copy(knew[:, :, 0:NQ], A.ka[:, :, bass.ds(SEQ + b * NQ, NQ)]).then_inc(new_k, 1)

        @block.tensor
        def _(pe):
            pe.sem_inc(turned, G)
            pe.sem_inc(v_used, G)
            pe.sem_inc(scored, 2)
            pe.wait_ge(qmade, 8)

            def keys(b):
                pe.wait_ge(w_ready, b + 1)
                for c0, c1 in banks:
                    pe.matmul(z[:, c0:c1], K.zeros16[:, 0:P], K.zeros16[:, 0:c1 - c0], start=True, stop=False,
                              skip_group_check=True)

                def score(k, page, f):
                    at = page * C + f * 8
                    return pe.matmul(z[:, at:at + 8], k, qnow[:, f, :], start=False, stop=False, skip_group_check=True)

                pe.wait_ge(new_q, b + 1)
                for page in range(NPG + 2):
                    side = page % 2
                    pe.wait_ge(evac[side], b * (NPG // 2) + page // 2 + 1)
                    if page < NPG:
                        pe.wait_ge(k_in[page % G], 16 * (b * NG + page // G + 1))
                        for f in range(HP):
                            last = pe.transpose(tp[side][:, f * P:(f + 1) * P], kring[:, page % G, f * P:(f + 1) * P], K.ident[:, :])
                        last.then_inc(turned, 1)
                    if page >= 2:
                        for f in range(HP):
                            last = score(kT[:, side, f * P:(f + 1) * P], page - 2, f)
                        last.then_inc(scored, 1)
                pe.wait_ge(new_k, b + 1)
                for f in range(HP):
                    last = score(knew[:, f, :], NPG, f)
                last.then_inc(z_ready, 1)

            def sums(b):
                pe.wait_ge(later_r, b + 1)
                for c0, c1 in banks:
                    last = pe.matmul(z[:, c0:c1], K.tri[:, :], soft[:, c0:c1], start=False, stop=True, skip_group_check=True)
                    if c0 < NPG * C:
                        last = pe.matmul(z[:, c0:c1], K.negones[:, :], later[:, c0 + C:c1 + C], start=False, stop=True,
                                         skip_group_check=True)
                last.then_inc(summed, 1)

            def values(b):
                pe.wait_ge(o_taken, b + 1)
                pe.wait_ge(w_masked, b + 1)
                for page in range(NPG):
                    pe.wait_ge(v_in[page % G], 16 * (b * NG + page // G + 1))
                    pe.matmul(o[0:C, :], wgt[:, page * C:(page + 1) * C], vring[:, page % G, :], start=page == 0, stop=False)\
                      .then_inc(v_used, 1)
                pe.wait_ge(new_v, 16 * (b + 1))
                pe.matmul(o[0:C, :], wgt[:, NPG * C:NP1 * C], vnew[:, :], start=False, stop=True).then_inc(o_ready, 1)
                pe.wait_ge(o_copied, b + 1)
                pe.sem_inc(pe_passed, 1)
                for f in range(HP):
                    last = pe.transpose(o2[:, f * C:(f + 1) * C], osb[:, f * P:(f + 1) * P], K.ident[0:C, 0:C])
                last.then_inc(o_turned, 1)

            keys(0)
            sums(0)
            with pe.Fori(1, NB) as b:
                keys(b)
                values(b - 1)
                sums(b)
            values(NB - 1)

        @block.scalar
        def _(act):
            act.preload_act_table_set("natural_log_exp_and_others")
            act.sem_inc(w_ready, 1)
            act.sem_inc(evac[0], 1)
            act.sem_inc(evac[1], 1)

            def take_keys(b):
                for page in range(NPG):
                    side = page % 2
                    act.wait_ge(turned, b * NPG + page + 1 + G)
                    act.wait_ge(scored, b * NPG + page + 1)
                    act.activation(kT[:, side, :], tp[side][:, :], ACT.Copy).then_inc(evac[side], 1)

            def weights(b):
                act.wait_ge(summed, b + 1)
                act.activation(wgt[:, 0:1024], z[:, 0:1024], ACT.Exp)
                act.activation(wgt[:, 1024:NP1 * C], z[:, 1024:NP1 * C], ACT.Exp).then_inc(w_ready, 1)

            def softplus(b):
                act.wait_ge(capped, b + 1)
                act.activation(expd[:, :], soft[:, :], ACT.Exp).then_inc(exp_r, 1)
                act.wait_ge(exp_r, b + 1)
                act.activation(expd[:, :], expd[:, :], ACT.Ln, bias=K.one[:, 0:1]).then_inc(ln_r, 1)

            take_keys(0)
            softplus(0)
            act.wait_ge(summed, 1)
            weights(0)
            with act.Fori(1, NB) as b:
                take_keys(b)
                softplus(b)
                weights(b)

        @block.vector
        def _(dve):
            dve.sem_inc(o_taken, 1)
            link = Link(dve, steps)
            shifts = (1, 2, 4, 8, 16, 32)
            ROUNDS = TOPK // 8 // NB
            PER = len(shifts) + 2 * ROUNDS

            def choose():
                for _ in range(ROUNDS):
                    dve.sem_inc(passed, 1)
                    link(dve.max(best[:, :], score))
                    dve.sem_inc(passed, 1)
                    link(dve.match_replace(score, best[:, :], score, LOW))


            def chain(b):
                dve.wait_ge(z_ready, b + 1)
                dve.tensor_scalar(soft[:, :], z[:, 0:NP1 * C], 40.0, None, ALU.min).then_inc(capped, 1)
                dve.wait_ge(ln_r, b + 1)
                link(dve.tensor_tensor(soft[:, :], expd[:, :], z[:, 0:NP1 * C], ALU.max))
                dve.tensor_tensor(soft[:, NPG * C:], soft[:, NPG * C:], ok[:, :], ALU.mult).then_inc(masked, 1)
                dve.wait_ge(masked, b + 1)
                src = soft
                for m, sh in enumerate(shifts):
                    w = (NP1 - sh) * C
                    if m == 0:
                        dve.tensor_copy(later[:, w:NP1 * C], soft[:, w:NP1 * C])
                    op = dve.tensor_tensor(later[:, 0:w], src[:, 0:w], src[:, sh * C:NP1 * C], ALU.add)
                    src = later
                    if m == len(shifts) - 1:
                        op.then_inc(later_r, 1)
                    else:
                        link(op)

            def mask_new(b):
                v = wgt[:, NPG * C:]
                dve.wait_ge(w_ready, b + 2)
                dve.tensor_tensor(v, v, bound[:, :], ALU.min).then_inc(w_masked, 1)

            def output(b):
                dve.wait_ge(o_ready, b + 1)
                dve.tensor_copy(osb[:, :], o[0:C, :]).then_inc(o_copied, 1)
                dve.wait_ge(o_turned, b + 1)
                for par in range(2):
                    rows = slice(par * DH, par * DH + DH)
                    for f in range(HP):
                        at = f * C + f * 8 + par * NQ
                        last = dve.tensor_copy(oT[rows, f, bass.ds(SEQ + b * NQ, NQ)], o2[rows, at:at + NQ])
                last.then_inc(o_taken, 1)

            dve.wait_ge(made, 7)
            for par in range(2):
                rows = slice(par * DH, par * DH + DH)
                for f in range(HP):
                    dve.tensor_copy(q[rows, f, :, par * NQ:par * NQ + NQ],
                                     A.qa[rows, f, SEQ:T].rearrange("p (b t) -> p b t", t=NQ)).then_inc(qmade, 1)
            choose()
            chain(0)
            mask_new(0)
            with dve.Fori(1, NB) as b:
                link.enter(b - 1, PER)
                choose()
                chain(b)
                output(b - 1)
                mask_new(b)
                link.leave(NB - 1, PER)
            output(NB - 1)


def stage_index_sample(nc, K, A, I):
    L = PAST + NQ
    G = 4
    NC = NPG // G
    CH = G * PAGE
    ic = I.cache_idx_k[0]
    n_pool = ic.shape[0]
    NR = 3
    order = [(c, b) for c in range(NC) for b in range(NB)]
    with Stage(nc, "sindex") as s:
        pages = s.sb("pages", [1, NB * NPG], I32)
        score = A.score
        ring = s.sb("ring", [P, NR, G, DH])
        kT = s.sb("kT", [P, 2, CH])
        relu = s.sb("relu", [NS, 2, CH])
        qi = s.sb("qi", [DH, NB, 8, NQ])
        wi8, pick8, pick4 = s.sb("wi8", [8, NS]), s.sb("pick8", [8, 8, NQ]), s.sb("pick4", [NQ, 8, NQ])
        wall, same = s.sb("wall", [NS, NS]), A.same
        wsel = s.sb("wsel", [NS, NB, NS])
        tp = [s.ps(f"tp{i}", [P, 512]) for i in range(2)]
        prod = [s.ps(f"prod{i}", [P, 512]) for i in range(2)]
        acc = [s.ps(f"acc{i}", [P, 512]) for i in range(2)]
        misc = s.ps("misc", [P, 512])
        (table, built, laid, small, small_taken, steps, turned, copied, product, relued, chunk_done, chunk_taken) = (
            s.sem(x) for x in ("table", "built", "laid", "small", "small_taken", "steps", "turned", "copied", "product",
                               "relued", "chunk_done", "chunk_taken"))
        arrived = [s.sem(f"arrived{i}") for i in range(NR)]
        block = s.block()
        N = len(order)

        @block.sync
        def _(sp):
            sp.dma_start(pages[:, :], I.page_table.rearrange("(o b) n -> o (b n)", o=1)).then_inc(table, 16)
            sp.wait_ge(table, 16)

            def load(n, b, c, cache, width, free):
                if free is not None:
                    sp.wait_ge(*free)
                numbers = page_numbers(nc, sp, pages, b * NPG + c * G, G, n_pool)
                for u in range(G):
                    sp.dma_start(ring[:, n % NR, u, 0:width], cache[bass.ds(numbers[u], 1)].rearrange("o p n -> p (o n)"))\
                      .then_inc(arrived[n % NR], 16)

            for n, (c, b) in enumerate(order):
                load(n, b, c, ic, DH, (turned, n - NR + 1) if n >= NR else None)

        @block.gpsimd
        def _(pool):
            for t in (pick8, pick4):
                pool.memset(t[:], 1.0).then_inc(built, 1)
            pool.memset(wsel[:], 0.0).then_inc(built, 1)
            pool.wait_ge(built, 3)
            for t, pattern, mul in ((pick8, [[-1, 8], [0, NQ]], 1), (pick4, [[0, 8], [-1, NQ]], 1)):
                pool.affine_select(out=t[:], in_=t[:], compare_op=ALU.is_equal, fill=0.0, base=0, pattern=pattern,
                                   channel_multiplier=mul).then_inc(built, 1)

        @block.tensor
        def _(pe):
            pe.wait_ge(built, 5)
            pe.transpose(misc[0:8, 0:NS], A.wtok[0:NS, NT, :], K.ident[0:NS, 0:NS]).then_inc(small, 1)
            pe.wait_ge(small_taken, 1)
            pe.matmul(misc[0:NS, 0:NS], pick8[:].rearrange("p h q -> p (h q)"), wi8[:, :], start=True, stop=True).then_inc(small, 1)
            pe.wait_ge(small_taken, 2)
            p4 = pick4[:].rearrange("p h q -> p (h q)")
            pe.matmul(misc[0:NS, 0:NS], p4, p4, start=True, stop=True).then_inc(small, 1)
            pe.wait_ge(small_taken, 3)
            pe.matmul(misc[0:NS, 0:NQ], p4, K.causal[0:NQ, 0:NQ], start=True, stop=True).then_inc(small, 1)
            pe.wait_ge(laid, 1)

            def turn(n, width):
                pe.wait_ge(arrived[n % NR], 16 * G * (n // NR + 1))
                if n >= 2:
                    pe.wait_ge(copied, n - 1)
                for u in range(G):
                    last = pe.transpose(tp[n % 2][0:width, u * P:(u + 1) * P], ring[:, n % NR, u, 0:width], K.ident[:, :])
                last.then_inc(turned, 1)

            def index_product(n, b, keys, cols):
                if n >= 2:
                    pe.wait_ge(relued, n - 1)
                pe.matmul(prod[n % 2][0:NS, 0:cols], qi[:, b, :, :].rearrange("p h q -> p (h q)"), keys,
                          start=True, stop=True).then_inc(product, 1)

            def index_sum(n, c, b, cols):
                pe.wait_ge(relued, n + 1)
                if b == 0 and c >= 2:
                    pe.wait_ge(chunk_taken, c - 1)
                last = pe.matmul(acc[c % 2][0:NS, 0:cols], wsel[:, b, :], relu[:, n % 2, 0:cols], start=(b == 0), stop=(b == NB - 1))
                last.then_inc(chunk_done, 1)

            for n, (c, b) in enumerate(order):
                turn(n, DH)
                if n >= 1:
                    pe.wait_ge(copied, n)
                    index_product(n - 1, order[n - 1][1], kT[0:DH, (n - 1) % 2, :], CH)
                if n >= 2:
                    index_sum(n - 2, *order[n - 2], CH)
            pe.wait_ge(copied, N)
            index_product(N - 1, NB - 1, kT[0:DH, (N - 1) % 2, :], CH)
            index_sum(N - 2, *order[N - 2], CH)
            index_sum(N - 1, *order[N - 1], CH)
            for b in range(NB):
                index_product(N + b, b, A.ki[0:DH, 0, SEQ + b * NQ:SEQ + (b + 1) * NQ], NQ)
                index_sum(N + b, NC, b, NQ)

        @block.scalar
        def _(act):
            act.preload_act_table_set("natural_log_exp_and_others")

            def copy_keys(n, width):
                act.wait_ge(turned, n + 1)
                if n < N and n >= 2:
                    act.wait_ge(product, n - 1)
                act.activation(kT[0:width, n % 2, :], tp[n % 2][0:width, :], ACT.Copy).then_inc(copied, 1)

            def relus(n, cols):
                act.wait_ge(product, n + 1)
                if n >= 2:
                    act.wait_ge(chunk_done, n - 1)
                act.activation(relu[:, n % 2, 0:cols], prod[n % 2][0:NS, 0:cols], ACT.Relu).then_inc(relued, 1)

            for n in range(N):
                copy_keys(n, DH)
                if n >= 1:
                    relus(n - 1, CH)
            relus(N - 1, CH)
            for b in range(NB):
                relus(N + b, NQ)

        @block.vector
        def _(dve):
            link = Link(dve, steps)
            dve.wait_ge(built, 5)
            dve.wait_ge(small, 1)
            dve.tensor_copy(wi8[:, :], misc[0:8, 0:NS]).then_inc(small_taken, 1)
            dve.wait_ge(small, 2)
            dve.tensor_copy(wall[:, :], misc[0:NS, 0:NS]).then_inc(small_taken, 1)
            dve.wait_ge(small, 3)
            dve.wait_ge(small_taken, 2)
            link(dve.tensor_tensor(wall[:, :], wall[:, :], misc[0:NS, 0:NS], ALU.mult))
            for b in range(NB):
                dve.tensor_copy(wsel[:, b, b * NQ:(b + 1) * NQ], wall[:, b * NQ:(b + 1) * NQ])
            for h in range(8):
                rows = slice((h % 2) * DH, (h % 2) * DH + DH)
                last = dve.tensor_copy(qi[:, :, h, :], A.qi[rows, h // 2, SEQ:T].rearrange("p (b q) -> p b q", q=NQ))
            last.then_inc(laid, 1)
            dve.sem_inc(small_taken, 1)
            dve.wait_ge(small, 4)
            link(dve.tensor_copy(same[:, 0:NQ], misc[0:NS, 0:NQ]))

            for c in range(NC + 1):
                dve.wait_ge(chunk_done, (c + 1) * NB)
                if c < NC:
                    dve.tensor_copy(score[0:NS, c * CH:(c + 1) * CH], acc[c % 2][0:NS, :]).then_inc(chunk_taken, 1)
                else:
                    dve.tensor_tensor(score[0:NS, PAST:L], acc[c % 2][0:NS, 0:NQ], same[:, 0:NQ], ALU.add).then_inc(chunk_taken, 1)


def stage_sparse_sample(nc, K, A, I, O, oT):
    L = PAST + NQ
    G = 4
    NC = NPG // G
    CH = G * PAGE
    kc = I.cache_dsa_k[0].rearrange("n p g d -> n p (g d)")
    vc = I.cache_dsa_v[0].rearrange("n p g d -> n p (g d)")
    n_pool = kc.shape[0]
    NR = 3
    order = [(c, b) for c in range(NC) for b in range(NB)]
    with Stage(nc, "ssparse") as s:
        pages = s.sb("pages", [1, NB * NPG], I32)
        turned_w = s.sb("turned_w", [P, (NPG + 1) * P])
        logit = [s.sb(f"logit{i}", [P, L]) for i in range(2)]
        spare = A.qa[:, :, :].rearrange("p t n -> p (t n)")
        ring = spare[:, 0:NR * G * P].rearrange("p (r u n) -> p r u n", r=NR, u=G)
        kT = s.sb("kT", [P, 2, CH])
        biasc = s.sb("biasc", [NS, 2, CH])
        qd = s.sb("qd", [P, NB, 2, HP, NQ])
        rep = s.sb("rep", [NS, NB, 8, NQ])
        vnew = spare[0:NQ, NR * G * P:(NR * G + NB) * P].rearrange("p (b n) -> p b n", b=NB)
        top, negtop, total, inv = (s.sb(x, [P, 2]) for x in ("top", "negtop", "total", "inv"))
        o_sb = s.sb("o_sb", [P, P])
        tp = [s.ps(f"tp{i}", [P, 512]) for i in range(2)]
        acc = [s.ps(f"acc{i}", [P, 512]) for i in range(2)]
        o = s.ps("o", [P, 512])
        misc = s.ps("misc", [P, 512])
        (table, built, laid, steps, turned, copied, biased, x_prod, x_taken, topped, exped, p_turned, p_taken, o_ready,
         o_scaled, o_turned, o_taken, new_v, v_used) = (s.sem(x) for x in (
             "table", "built", "laid", "steps", "turned", "copied", "biased", "x_prod", "x_taken", "topped", "exped",
             "p_turned", "p_taken", "o_ready", "o_scaled", "o_turned", "o_taken", "new_v", "v_used"))
        arrived = [s.sem(f"arrived{i}") for i in range(NR)]
        block = s.block()
        N = len(order)

        @block.sync
        def _(sp):
            sp.dma_start(pages[:, :], I.page_table.rearrange("(o b) n -> o (b n)", o=1)).then_inc(table, 16)
            sp.dma_start(vnew[:, :, :], O.dsa_v_s[0].rearrange("b t g d -> t b (g d)")).then_inc(new_v, 16)
            sp.wait_ge(table, 16)

            def load(n, b, c, cache, width, free):
                if free is not None:
                    sp.wait_ge(*free)
                numbers = page_numbers(nc, sp, pages, b * NPG + c * G, G, n_pool)
                for u in range(G):
                    sp.dma_start(ring[:, n % NR, u, 0:width], cache[bass.ds(numbers[u], 1)].rearrange("o p n -> p (o n)"))\
                      .then_inc(arrived[n % NR], 16)

            for n, (c, b) in enumerate(order):
                load(n, b, c, kc, P, (turned, n - NR + 1) if n >= NR else None)
            for m in range(N):
                hb, c, b4 = m // (NC * 4), m % (NC * 4) // 4, m % 4
                n = N + m
                load(n, hb * 4 + b4, c, vc, P, (turned, n - NR + 1) if m < NR else (v_used, m - NR + 1))

        @block.gpsimd
        def _(pool):
            pool.memset(rep[:], 1.0).then_inc(built, 1)
            pool.memset(qd[:], 0.0).then_inc(built, 1)
            pool.wait_ge(built, 2)
            pool.affine_select(out=rep[:], in_=rep[:], compare_op=ALU.is_equal, fill=0.0, base=0,
                               pattern=[[-NQ, NB], [0, 8], [-1, NQ]], channel_multiplier=1).then_inc(built, 1)

        @block.tensor
        def _(pe):
            pe.wait_ge(built, 3)
            pe.wait_ge(laid, 1)

            def turn(n, width):
                pe.wait_ge(arrived[n % NR], 16 * G * (n // NR + 1))
                if n >= 2:
                    pe.wait_ge(copied, n - 1)
                for u in range(G):
                    last = pe.transpose(tp[n % 2][0:width, u * P:(u + 1) * P], ring[:, n % NR, u, 0:width], K.ident[:, :])
                last.then_inc(turned, 1)

            def logits(m, c, b, keys, cols):
                half, row = b // 4, (b % 4) * NS
                if b % 4 == 0 and c >= 1:
                    pe.wait_ge(x_taken, 2 * (c - 1) + half + 1)
                if b == 0:
                    pe.wait_ge(biased, c + 1)
                dst = acc[half][row:row + NS, 0:cols]
                pe.matmul(dst, qd[:, b].rearrange("p g r q -> p (g r q)"), keys, start=True, stop=False)
                pe.matmul(dst, rep[:, b].rearrange("p x q -> p (x q)"), biasc[:, c % 2, 0:cols], start=False, stop=True).then_inc(x_prod, 1)

            for m, (c, b) in enumerate(order):
                turn(m, P)
                if m >= 1:
                    pe.wait_ge(copied, m)
                    logits(m - 1, *order[m - 1], kT[:, (m - 1) % 2, :], CH)
            pe.wait_ge(copied, N)
            logits(N - 1, *order[N - 1], kT[:, (N - 1) % 2, :], CH)
            for b in range(NB):
                logits(N + b, NC, b, A.kb[:, 0, SEQ + b * NQ:SEQ + (b + 1) * NQ], NQ)

            for half in range(2):
                pe.wait_ge(exped, half + 1)
                for g in range(NC + 1):
                    n = half * (NC + 1) + g
                    if n >= 2:
                        pe.wait_ge(p_taken, n - 1)
                    if n < 2:
                        pe.wait_ge(copied, N)
                    for u in range(G if g < NC else 1):
                        at = (g * G + u) * P
                        w = min(P, L - at)
                        last = pe.transpose(tp[n % 2][0:w, u * P:(u + 1) * P], logit[half][:, at:at + w], K.ident[:, :])
                    last.then_inc(p_turned, 1)
                if half == 1:
                    pe.wait_ge(o_scaled, 1)
                for g in range(NC + 1):
                    pe.wait_ge(p_taken, half * (NC + 1) + g + 1)
                    for b4 in range(4):
                        b = half * 4 + b4
                        dst = o[b4 * NS:(b4 + 1) * NS, 0:P]
                        if g == NC:
                            pe.wait_ge(new_v, 16)
                            last = pe.matmul(dst, turned_w[0:NQ, NPG * P + b4 * NS:NPG * P + (b4 + 1) * NS], vnew[:, b, :],
                                             start=False, stop=True)
                            continue
                        m = half * NC * 4 + g * 4 + b4
                        n = N + m
                        pe.wait_ge(arrived[n % NR], 16 * G * (n // NR + 1))
                        for u in range(G):
                            at = (g * G + u) * P + b4 * NS
                            last = pe.matmul(dst, turned_w[:, at:at + NS], ring[:, n % NR, u, :],
                                             start=(g == 0 and u == 0), stop=False)
                        last.then_inc(v_used, 1)
                last.then_inc(o_ready, 1)
                pe.wait_ge(o_scaled, half + 1)
                pe.transpose(misc[:, 0:P], o_sb[:, :], K.ident[:, :]).then_inc(o_turned, 1)

        @block.scalar
        def _(act):
            act.preload_act_table_set("natural_log_exp_and_others")

            def copy_keys(n, width):
                act.wait_ge(turned, n + 1)
                if n >= 2:
                    act.wait_ge(x_prod, n - 1)
                act.activation(kT[0:width, n % 2, :], tp[n % 2][0:width, :], ACT.Copy).then_inc(copied, 1)

            def take(c, half, cols):
                act.wait_ge(x_prod, c * NB + half * 4 + 4)
                act.activation(logit[half][:, c * CH:c * CH + cols], acc[half][:, 0:cols], ACT.Copy).then_inc(x_taken, 1)

            for m in range(N):
                copy_keys(m, P)
                c, b = order[m]
                if m >= 4 and b in (1, 5):
                    take(c - 1 if b == 1 else c, 1 if b == 1 else 0, CH) if not (b == 1 and c == 0) else None
            take(NC - 1, 1, CH)
            take(NC, 0, NQ)
            take(NC, 1, NQ)
            for half in range(2):
                act.wait_ge(topped, half + 1)
                act.activation(logit[half][:, :], logit[half][:, :], ACT.Exp, bias=negtop[:, half:half + 1], scale=DH ** -0.5,
                               accum_out=total[:, half:half + 1]).then_inc(exped, 1)

        @block.vector
        def _(dve):
            link = Link(dve, steps)
            dve.wait_ge(built, 3)
            for g in range(2):
                rows = slice(g * DH, (g + 1) * DH)
                for b in range(NB):
                    last = dve.tensor_copy(qd[rows, b, g, :, :], A.qb[rows, :, SEQ + b * NQ:SEQ + (b + 1) * NQ])
            last.then_inc(laid, 1)
            for c in range(NC + 1):
                cols = CH if c < NC else NQ
                if c >= 2:
                    dve.wait_ge(x_prod, (c - 1) * NB)
                op = dve.tensor_scalar(biasc[:, c % 2, 0:cols], A.score[0:NS, c * CH:c * CH + cols], LOW / 2, FILL, ALU.is_gt, ALU.mult)
                if c == NC:
                    link(op)
                    op = dve.tensor_tensor(biasc[:, c % 2, 0:cols], biasc[:, c % 2, 0:cols], A.same[:, 0:NQ], ALU.add)
                op.then_inc(biased, 1)
            for half in range(2):
                dve.wait_ge(x_taken, 2 * NC + half + 1)
                link(dve.tensor_reduce(top[:, half:half + 1], logit[half][:, :], AX.X, ALU.max))
                dve.tensor_scalar(negtop[:, half:half + 1], top[:, half:half + 1], -(DH ** -0.5), None, ALU.mult).then_inc(topped, 1)
            for half in range(2):
                if half == 1:
                    dve.wait_ge(o_ready, 1)
                for g in range(NC + 1):
                    n = half * (NC + 1) + g
                    dve.wait_ge(p_turned, n + 1)
                    if g < NC:
                        dve.tensor_copy(turned_w[:, g * CH:(g + 1) * CH], tp[n % 2][:, :]).then_inc(p_taken, 1)
                    else:
                        dve.tensor_copy(turned_w[0:NQ, NPG * P:(NPG + 1) * P], tp[n % 2][0:NQ, 0:P]).then_inc(p_taken, 1)
                dve.wait_ge(exped, half + 1)
                link(dve.reciprocal(inv[:, half:half + 1], total[:, half:half + 1]))
                dve.wait_ge(o_ready, half + 1)
                dve.tensor_scalar(o_sb[:, :], o[:, 0:P], inv[:, half:half + 1], None, ALU.mult).then_inc(o_scaled, 1)
                dve.wait_ge(o_turned, half + 1)
                for g in range(2):
                    rows = slice(g * DH, (g + 1) * DH)
                    for b4 in range(4):
                        at = SEQ + (half * 4 + b4) * NQ
                        c0 = b4 * NS + g * HP * NQ
                        last = dve.tensor_copy(oT[rows, HP:2 * HP, at:at + NQ],
                                               misc[rows, c0:c0 + HP * NQ].rearrange("p (r q) -> p r q", q=NQ))
                last.then_inc(o_taken, 1)


def stage_linear(nc, K, name, src, kt, loads, n, dst, act_fn=None):
    per = min(n, 2)
    with Stage(nc, name) as s:
        w = [s.sb(f"w{u}", [P, kt, P]) for u in range(per)]
        acc = [s.ps(f"acc{u}", [P, NCH, 512]) for u in range(per)]
        w_loaded = [s.sem(f"w_loaded{u}") for u in range(per)]
        product, taken = s.sem("product"), s.sem("taken")
        n_loads = len(loads(0))
        block = s.block()

        @block.sync
        def _(sp):
            with sp.Fori(0, n // per) as i:
                for u in range(per):
                    sp.wait_ge(product, per * i + u + 1)
                    for dram, rows, ks in loads(per * i + u):
                        sp.dma_start(w[u][rows, ks, :], dram).then_inc(w_loaded[u], 16)

        @block.tensor
        def _(pe):
            pe.sem_inc(product, per)
            with pe.Fori(0, n // per) as i:
                for u in range(per):
                    pe.wait_ge(w_loaded[u], 16 * n_loads * (i + 1))
                    pe.wait_ge(taken, per * i + u + 1)
                    for c in range(NCH):
                        for k in range(kt):
                            last = pe.matmul(acc[u][:, c, 0:CW], w[u][:, k, :], src[:, k, c * CW:(c + 1) * CW],
                                             start=(k == 0), stop=(k == kt - 1))
                    last.then_inc(product, 1)

        @block.vector
        def _(dve):
            dve.sem_inc(taken, per)
            with dve.Fori(0, n // per) as i:
                for u in range(per):
                    dve.wait_ge(product, per * i + u + 1 + per)
                    out = dst[:, bass.ds(per * i + u, 1), :].rearrange("p o (c n) -> p (o c) n", c=NCH)
                    dve.tensor_copy(out, chunks(acc[u])).then_inc(taken, 1)


def column_loads(w, kt):
    W = w.rearrange("(k p) n -> p k n", p=P)
    return lambda i: [(W[:, :, bass.ds(i * P, P)], slice(0, P), slice(0, kt))]


def attention_out_loads(w):
    W = w[0:HP * P].rearrange("(k p) n -> p k n", p=P)
    S = w[HP * P:].rearrange("(g r d) n -> g d r n", g=2, r=HP)
    return lambda i: [(W[:, :, bass.ds(i * P, P)], slice(0, P), slice(0, HP)),
                      (S[0][:, :, bass.ds(i * P, P)], slice(0, DH), slice(HP, 2 * HP)),
                      (S[1][:, :, bass.ds(i * P, P)], slice(DH, P), slice(HP, 2 * HP))]


def stage_ffn_prepare(nc, K, name, conv_w, conv_b, state, taps, stateT, scratch):
    M = 2 * KF
    with Stage(nc, name) as s:
        rows = s.sb("rows", [M, 4, P])
        tp = s.ps("tp", [P, 4, M])
        tq = s.ps("tq", [P, 2, 512])
        loaded, turned, taken = s.sem("loaded"), s.sem("turned"), s.sem("taken")
        block = s.block()

        @block.sync
        def _(sp):
            sp.dma_start(rows[:, 0:3, :], conv_w.rearrange("j (m p) -> m j p", p=P)).then_inc(loaded, 16)
            sp.dma_start(rows[:, 3, :], conv_b.rearrange("(m p) -> m p", p=P)).then_inc(loaded, 16)
            sp.dma_start(scratch, state.rearrange("b w n -> (b w) n")).then_inc(loaded, 16)

        @block.tensor
        def _(pe):
            pe.wait_ge(loaded, 48)
            for j in range(4):
                pe.transpose(tp[:, j, :], rows[:, j, :], K.ident[0:M, 0:M])
            for m in range(M):
                last = pe.transpose(tq[:, m // KF, m % KF * 16:m % KF * 16 + 16], scratch[:, m * P:(m + 1) * P], K.ident[0:16, 0:16])
            last.then_inc(turned, 1)

        @block.vector
        def _(dve):
            dve.wait_ge(turned, 1)
            dve.tensor_copy(taps[:, :, :], tp[:, :, :])
            dve.tensor_copy(stateT.rearrange("p (u m) n -> p u (m n)", u=2), tq[:, :, 0:KF * 16]).then_inc(taken, 1)


def stage_ffn_up(nc, K, name, w_up, hT, taps, stateT, last_u, hidden):
    W = w_up.rearrange("(k p) n -> p k n", p=P)
    UW = 2 + SEQ + NB * 6
    CO = UW - 2
    S0 = 2 + SEQ
    SP2 = SEQ - 2 * CW

    with Stage(nc, name) as s:
        w = [s.sb(f"w{u}", [P, KD, P]) for u in range(2)]
        ubuf = [s.sb(f"u{u}", [P, UW]) for u in range(2)]
        cbuf = [s.sb(f"c{u}", [P, UW]) for u in range(2)]
        acc = [s.ps(f"acc{u}", [P, NCH, 512]) for u in range(2)]
        w_loaded = [s.sem(f"w_loaded{u}") for u in range(2)]
        product, evacuated, conved, gelued, steps, zeroed = (s.sem(x) for x in (
            "product", "evacuated", "conved", "gelued", "steps", "zeroed"))
        block = s.block()

        def per_seq(ap, a, b):
            return ap.rearrange("p (b t) -> p b t", b=NB)[:, :, a:b]

        @block.sync
        def _(sp):
            with sp.Fori(0, KF) as j:
                for u in range(2):
                    sp.wait_ge(product, 2 * j + u + 1)
                    sp.dma_start(w[u][:, :, :], W[:, :, bass.ds(j * P + u * D_FF, P)]).then_inc(w_loaded[u], 16)

        @block.tensor
        def _(pe):
            pe.sem_inc(product, 2)
            with pe.Fori(0, KF) as j:
                for u in range(2):
                    pe.wait_ge(w_loaded[u], 16 * (j + 1))
                    pe.wait_ge(evacuated, 2 * j + u + 1)
                    for c in range(NCH):
                        for k in range(KD):
                            last = pe.matmul(acc[u][:, c, 0:CW], w[u][:, k, :], hT[:, k, c * CW:(c + 1) * CW],
                                             start=(k == 0), stop=(k == KD - 1))
                    last.then_inc(product, 1)

        @block.scalar
        def _(act):
            act.wait_ge(zeroed, 2)
            act.sem_inc(evacuated, 2)
            with act.Fori(0, KF) as j:
                for u in range(2):
                    m = bass.ds(j + u * KF, 1)
                    act.wait_ge(product, 2 * j + u + 3)
                    act.wait_ge(conved, 2 * j + u + 1)
                    act.activation(ubuf[u][:, 2:2 + 2 * CW].rearrange("p (c n) -> p c n", c=2), acc[u][:, 0:2, 0:CW], ACT.Copy)
                    act.activation(ubuf[u][:, 2 + 2 * CW:S0], acc[u][:, 2, 0:SP2], ACT.Copy)
                    new = acc[u][:, 2, SP2:CW]
                    act.activation(per_seq(ubuf[u][:, S0:UW], 2, 6), new.rearrange("p (b t) -> p b t", b=NB), ACT.Copy)
                    act.activation(per_seq(ubuf[u][:, S0:UW], 0, 2), stateT[:, m, :].rearrange("p o (b t) -> p (o b) t", b=NB), ACT.Copy)
                    act.activation(last_u[:, m, 0:2], acc[u][:, 2, SP2 - 2:SP2].rearrange("p (o t) -> p o t", o=1), ACT.Copy)
                    act.activation(last_u[:, m, 2:18].rearrange("p o (b t) -> p (o b) t", b=NB), per_seq(new, 2, 4), ACT.Copy)\
                       .then_inc(evacuated, 1)
                act.wait_ge(conved, 2 * j + 3)
                act.activation(cbuf[0][:, 0:CO], cbuf[0][:, 0:CO], ACT.Gelu_apprx_tanh).then_inc(gelued, 1)

        @block.vector
        def _(dve):
            for u in range(2):
                dve.memset(ubuf[u][:, 0:2], 0.0).then_inc(zeroed, 1)
            dve.sem_inc(conved, 2)
            link = Link(dve, steps)
            with dve.Fori(0, KF) as j:
                link.enter(j, 8)
                for u in range(2):
                    m = bass.ds(j + u * KF, 1)
                    tap = [taps[:, i, m] for i in range(4)]
                    dve.wait_ge(evacuated, 2 * j + u + 3)
                    c = cbuf[u][:, 0:CO]
                    link(dve.tensor_scalar(c, ubuf[u][:, 0:CO], tap[0], tap[3], ALU.mult, ALU.add))
                    link(dve.scalar_tensor_tensor(out=c, in0=ubuf[u][:, 1:1 + CO], scalar=tap[1], in1=c, op0=ALU.mult, op1=ALU.add))
                    link(dve.scalar_tensor_tensor(out=c, in0=ubuf[u][:, 2:2 + CO], scalar=tap[2], in1=c, op0=ALU.mult, op1=ALU.add))
                    dve.sem_inc(conved, 1)
                dve.wait_ge(gelued, j + 1)
                out = hidden[:, bass.ds(j, 1), :].rearrange("p o t -> p (o t)")
                link(dve.tensor_tensor(out[:, 0:SEQ], cbuf[0][:, 0:SEQ], cbuf[1][:, 0:SEQ], ALU.mult))
                link(dve.tensor_tensor(out[:, SEQ:T].rearrange("p (b t) -> p b t", b=NB), per_seq(cbuf[0][:, S0:UW], 0, 4),
                                       per_seq(cbuf[1][:, S0:UW], 0, 4), ALU.mult))
            link.leave(KF, 8)


def stage_ffn_state(nc, K, name, last_u, out_p, out_s, rows):
    M = 2 * KF
    with Stage(nc, name) as s:
        tp = [s.ps(f"tp{i}", [18, 4, P]) for i in range(2)]
        turned, taken, stored = s.sem("turned"), s.sem("taken"), s.sem("stored")
        block = s.block()

        @block.tensor
        def _(pe):
            for g in range(M // 4):
                if g >= 2:
                    pe.wait_ge(taken, g - 1)
                for m in range(4):
                    last = pe.transpose(tp[g % 2][:, m, :], last_u[:, g * 4 + m, :], K.ident[:, :])
                last.then_inc(turned, 1)

        @block.vector
        def _(dve):
            for g in range(M // 4):
                dve.wait_ge(turned, g + 1)
                dve.tensor_copy(rows[0:18, g * 512:(g + 1) * 512], tp[g % 2][:, :, :].rearrange("p m n -> p (m n)")).then_inc(taken, 1)

        @block.sync
        def _(sp):
            sp.wait_ge(taken, M // 4)
            sp.dma_start(out_p.rearrange("b w n -> (b w) n"), rows[0:2, 0:2 * D_FF]).then_inc(stored, 16)
            sp.dma_start(out_s.rearrange("b w n -> (b w) n"), rows[2:18, 0:2 * D_FF]).then_inc(stored, 16)
            sp.wait_ge(stored, 32)


def ffn(nc, K, I, O, layer, x, h):
    with ExitStack() as c:
        hidden = c.enter_context(nc.sbuf_tensor(f"hidden{layer}", [P, KF, T], F32))
        taps = c.enter_context(nc.sbuf_tensor(f"taps{layer}", [P, 4, 2 * KF], F32))
        stateT = c.enter_context(nc.sbuf_tensor(f"stateT{layer}", [P, 2 * KF, 16], F32))
        last_u = c.enter_context(nc.sbuf_tensor(f"last_u{layer}", [P, 2 * KF, 18], F32))
        flat = hidden[:, :, :].rearrange("p k t -> p (k t)")
        stage_norm(nc, K, f"fpre{layer}", x, I.norm_ffn_pre[layer], h)
        stage_ffn_prepare(nc, K, f"fprep{layer}", I.ffn_conv_w[layer], I.ffn_conv_b[layer], I.state_ffn_conv[layer],
                          taps, stateT[:, :, :], flat[0:16, 0:2 * D_FF])
        stage_ffn_up(nc, K, f"fup{layer}", I.ffn_w_up[layer], h, taps, stateT, last_u, hidden)
        stage_ffn_state(nc, K, f"fstate{layer}", last_u, O.ffn_conv_p[layer], O.ffn_conv_s[layer],
                        h[:, :, :].rearrange("p k t -> p (k t)"))
        stage_linear(nc, K, f"fdown{layer}", hidden, KF, column_loads(I.ffn_w_down[layer], KF), KD, h)
        stage_norm(nc, K, f"fpost{layer}", h, I.norm_ffn_post[layer], h, residual=x, square=hidden)


def stage_reload(nc, name, dram, sbuf):
    with Stage(nc, name) as s:
        loaded = s.sem("loaded")
        block = s.block()

        @block.sync
        def _(sp):
            sp.dma_start(sbuf[:, :, :], dram).then_inc(loaded, 16)
            sp.wait_ge(loaded, 16)


def stage_y(nc, K, name, x, out_p, out_s):
    with Stage(nc, name) as s:
        rows = s.sb("rows", [P, 2, D])
        tp = [s.ps(f"tp{i}", [P, KD, P]) for i in range(2)]
        turned, taken = s.sem("turned"), s.sem("taken")
        stored = [s.sem(f"stored{i}") for i in range(2)]
        block = s.block()

        @block.tensor
        def _(pe):
            for t in range(NT + 1):
                n = P if t < NT else NS
                if t >= 2:
                    pe.wait_ge(taken, t - 1)
                for k in range(KD):
                    last = pe.transpose(tp[t % 2][0:n, k, :], x[:, k, t * P:t * P + n], K.ident[:, :])
                last.then_inc(turned, 1)

        @block.vector
        def _(dve):
            for t in range(NT + 1):
                n = P if t < NT else NS
                dve.wait_ge(turned, t + 1)
                if t >= 2:
                    dve.wait_ge(stored[t % 2], 16 * (t // 2))
                dve.tensor_copy(rows[0:n, t % 2, :], tp[t % 2][0:n, :, :].rearrange("p k n -> p (k n)")).then_inc(taken, 1)

        @block.sync
        def _(sp):
            for t in range(NT + 1):
                sp.wait_ge(taken, t + 1)
                if t < NT:
                    sp.dma_start(out_p[0, t * P:(t + 1) * P, :], rows[:, t % 2, :]).then_inc(stored[t % 2], 16)
                else:
                    sp.dma_start(out_s.rearrange("b t d -> (b t) d"), rows[0:NS, t % 2, :]).then_inc(stored[t % 2], 16)
            sp.wait_ge(stored[0], 80)
            sp.wait_ge(stored[1], 64)


VECTORS = ("mix0", "mix1", "mix2", "mix3", "mix4", "mix5", "w0", "a0", "k_k", "k_a", "r_k", "ln_w", "ln_b")
CHUNK = 64
NLV = 6
DECAY = -0.6065306597126334


def fill_halves(pool, halves, filled):
    pool.memset(halves[:, :], 0.0).then_inc(filled, 1)
    pool.wait_ge(filled, 1)
    for q in range(2):
        pool.memset(halves[q * DH:(q + 1) * DH, q * DH:(q + 1) * DH], 1.0).then_inc(filled, 1)


def stage_rwkv_vectors(nc, K, I, h, V, prev, O):
    n_vec = len(VECTORS)
    with Stage(nc, "vec") as s:
        rows = s.sb("rows", [n_vec * KD, P])
        state = s.sb("state", [NB, D])
        last_row = s.sb("last_row", [1 + NB, D])
        ends = s.sb("ends", [P, KD, 1 + NB])
        tp = s.ps("tp", [P, n_vec * KD])
        tq = s.ps("tq", [P, KD, NB])
        tr = s.ps("tr", [1 + NB, KD, P])
        loaded, turned, taken, picked, stored = (s.sem(x) for x in ("loaded", "turned", "taken", "picked", "stored"))
        block = s.block()
        src = [I.rk_mix[0][j] for j in range(6)] + [x[0] for x in (I.rk_w0, I.rk_a0, I.rk_k_k, I.rk_k_a)]
        src += [I.rk_r_k[0].rearrange("h n -> (h n)"), I.rk_ln_w[0], I.rk_ln_b[0]]

        @block.sync
        def _(sp):
            for j, v in enumerate(src):
                sp.dma_start(rows[j * KD:(j + 1) * KD, :], v.rearrange("(k p) -> k p", p=P)).then_inc(loaded, 16)
            sp.dma_start(state[:, :], I.state_shift[0]).then_inc(loaded, 16)
            sp.wait_ge(taken, 3)
            sp.dma_start(O.shift_p[0], last_row[0:1, :]).then_inc(stored, 16)
            sp.dma_start(O.shift_s[0], last_row[1:1 + NB, :]).then_inc(stored, 16)
            sp.wait_ge(stored, 32)

        @block.tensor
        def _(pe):
            pe.wait_ge(loaded, 16 * (n_vec + 1))
            pe.wait_ge(picked, 2)
            pe.transpose(tp[:, :], rows[:, :], K.ident[0:n_vec * KD, 0:n_vec * KD]).then_inc(turned, 1)
            for k in range(KD):
                last = pe.transpose(tq[:, k, :], state[:, k * P:(k + 1) * P], K.ident[0:NB, 0:NB])
            last.then_inc(turned, 1)
            for k in range(KD):
                last = pe.transpose(tr[:, k, :], ends[:, k, :], K.ident[:, :])
            last.then_inc(turned, 1)

        @block.vector
        def _(dve):
            dve.tensor_copy(ends[:, :, 0:1], h[:, :, SEQ - 1:SEQ]).then_inc(picked, 1)
            dve.tensor_copy(ends[:, :, 1:1 + NB].unsqueeze(3), h[:, :, SEQ:T].rearrange("p k (b t) -> p k b t", b=NB)[:, :, :, NQ - 1:NQ])\
               .then_inc(picked, 1)
            dve.wait_ge(turned, 3)
            dve.tensor_copy(V[:, :, :].rearrange("p j k -> p (j k)"), tp[:, :]).then_inc(taken, 1)
            dve.tensor_copy(prev[:, :, :], tq[:, :, :]).then_inc(taken, 1)
            dve.tensor_copy(last_row[:, :], tr[:, :, :].rearrange("p k n -> p (k n)")).then_inc(taken, 1)


def stage_shift(nc, K, h, prev, xx):
    with Stage(nc, "shift") as s:
        done = s.sem("done")
        block = s.block()

        @block.vector
        def _(dve):
            for k in range(KD):
                hs, xs = (t[:, k, SEQ:T].rearrange("p (b t) -> p b t", b=NB) for t in (h, xx))
                dve.tensor_tensor(xx[:, k, 1:SEQ], h[:, k, 0:SEQ - 1], h[:, k, 1:SEQ], ALU.subtract)
                dve.tensor_scalar(xx[:, k, 0:1], h[:, k, 0:1], -1.0, None, ALU.mult)
                dve.tensor_tensor(xs[:, :, 1:NQ], hs[:, :, 0:NQ - 1], hs[:, :, 1:NQ], ALU.subtract)
                dve.tensor_tensor(xs[:, :, 0:1], prev[:, k, :].unsqueeze(2), hs[:, :, 0:1], ALU.subtract).then_inc(done, 1)
            dve.wait_ge(done, KD)


def stage_mix(nc, K, j, h, xx, V, m):
    with Stage(nc, f"mix{j}") as s:
        done = s.sem("done")
        block = s.block()

        @block.vector
        def _(dve):
            for k in range(KD):
                dve.scalar_tensor_tensor(out=m[:, k, :], in0=xx[:, k, :], scalar=V[:, j, k:k + 1], in1=h[:, k, :],
                                         op0=ALU.mult, op1=ALU.add).then_inc(done, 1)
            dve.wait_ge(done, KD)


def stage_lora(nc, K, name, m, first, second, rank, inner, bias, outer, dst):
    parts = [(a, min(P, rank - a)) for a in range(0, rank, P)]
    with Stage(nc, name) as s:
        w1 = s.sb("w1", [P, KD, rank])
        w2 = s.sb("w2", [P, len(parts), D])
        t = s.sb("t", [P, len(parts), T])
        acc = [s.ps(f"acc{i}", [P, NCH, 512]) for i in range(2)]
        loaded, product, taken = s.sem("loaded"), s.sem("product"), s.sem("taken")
        block = s.block()
        NPT = len(parts)

        @block.sync
        def _(sp):
            sp.dma_start(w1[:, :, :], first.rearrange("(k p) n -> p k n", p=P)).then_inc(loaded, 16)
            for i, (a, n) in enumerate(parts):
                sp.dma_start(w2[0:n, i, :], second[a:a + n]).then_inc(loaded, 16)

        @block.tensor
        def _(pe):
            pe.wait_ge(loaded, 16 * (1 + NPT))
            for i, (a, n) in enumerate(parts):
                for c in range(NCH):
                    for k in range(KD):
                        last = pe.matmul(acc[i % 2][0:n, c, 0:CW], w1[:, k, a:a + n], m[:, k, c * CW:(c + 1) * CW],
                                         start=(k == 0), stop=(k == KD - 1))
                last.then_inc(product, 1)
            pe.wait_ge(taken, NPT)
            for o in range(KD):
                u = NPT + o
                if u >= 2:
                    pe.wait_ge(taken, u - 1)
                for c in range(NCH):
                    for i, (a, n) in enumerate(parts):
                        last = pe.matmul(acc[u % 2][:, c, 0:CW], w2[0:n, i, o * P:(o + 1) * P], t[0:n, i, c * CW:(c + 1) * CW],
                                         start=(i == 0), stop=(i == NPT - 1))
                last.then_inc(product, 1)

        @block.scalar
        def _(act):
            for i, (a, n) in enumerate(parts):
                act.wait_ge(product, i + 1)
                act.activation(row3(t[0:n, i, :]), acc[i % 2][0:n, :, 0:CW], inner).then_inc(taken, 1)
            for o in range(KD):
                u = NPT + o
                act.wait_ge(product, u + 1)
                b = {} if bias is None else {"bias": bias[:, o:o + 1]}
                act.activation(row3(dst[:, o, :]), chunks(acc[u % 2]), outer, **b).then_inc(taken, 1)
            act.wait_ge(taken, NPT + KD)


def stage_keep(nc, K, name, src, dram, dram_new, scale=None):
    with Stage(nc, name) as s:
        rows = s.sb("rows", [NS, D])
        tp = s.ps("tp", [NS, KD, P])
        scaled, turned, taken, stored = s.sem("scaled"), s.sem("turned"), s.sem("taken"), s.sem("stored")
        block = s.block()

        @block.scalar
        def _(act):
            if scale is not None:
                for k in range(KD):
                    act.activation(src[:, k, :], src[:, k, :], ACT.Copy, scale=scale).then_inc(scaled, 1)

        @block.tensor
        def _(pe):
            if dram_new is None:
                return
            if scale is not None:
                pe.wait_ge(scaled, KD)
            for k in range(KD):
                last = pe.transpose(tp[:, k, :], src[:, k, SEQ:T], K.ident[:, :])
            last.then_inc(turned, 1)

        @block.vector
        def _(dve):
            if dram_new is None:
                return
            dve.wait_ge(turned, 1)
            dve.tensor_copy(rows[:, :], tp[:, :, :].rearrange("p k n -> p (k n)")).then_inc(taken, 1)

        @block.sync
        def _(sp):
            if scale is not None:
                sp.wait_ge(scaled, KD)
            sp.dma_start(dram, src[:, :, :]).then_inc(stored, 16)
            if dram_new is not None:
                sp.wait_ge(taken, 1)
                sp.dma_start(dram_new, rows[:, :]).then_inc(stored, 16)
            sp.wait_ge(stored, 16 if dram_new is None else 32)


def stage_keys(nc, K, V, k_, a_, kk, bb):
    VK, VA = VECTORS.index("k_k"), VECTORS.index("k_a")
    with Stage(nc, "keys") as s:
        norm = [s.sb(f"norm{i}", [P, T]) for i in range(2)]
        total = [s.ps(f"total{i}", [P, NCH, 512]) for i in range(2)]
        halves = s.sb("halves", [P, P])
        squared, summed, rooted, steps, filled = (s.sem(x) for x in ("squared", "summed", "rooted", "steps", "filled"))
        block = s.block()

        @block.gpsimd
        def _(pool):
            fill_halves(pool, halves, filled)

        @block.tensor
        def _(pe):
            pe.wait_ge(filled, 3)
            for k in range(KD):
                pe.wait_ge(squared, k + 1)
                if k >= 2:
                    pe.wait_ge(rooted, k - 1)
                for c in range(NCH):
                    last = pe.matmul(total[k % 2][:, c, 0:CW], halves[:, :], bb[:, k, c * CW:(c + 1) * CW], start=True, stop=True)
                last.then_inc(summed, 1)

        @block.scalar
        def _(act):
            for k in range(KD):
                act.wait_ge(summed, k + 1)
                if k >= 2:
                    act.wait_ge(steps, KD + 5 * (k - 1))
                act.activation(row3(norm[k % 2][:, :]), chunks(total[k % 2]), ACT.Sqrt).then_inc(rooted, 1)

        @block.vector
        def _(dve):
            link = Link(dve, steps)
            for k in range(KD):
                link(dve.tensor_scalar(kk[:, k, :], k_[:, k, :], V[:, VK, k:k + 1], None, ALU.mult))
                dve.tensor_tensor(bb[:, k, :], kk[:, k, :], kk[:, k, :], ALU.mult).then_inc(squared, 1)
            dve.wait_ge(squared, KD)
            for k in range(KD):
                n = norm[k % 2][:, :]
                dve.wait_ge(rooted, k + 1)
                link(dve.tensor_scalar(n, n, 1e-12, None, ALU.max))
                link(dve.reciprocal(n, n))
                link(dve.tensor_tensor(kk[:, k, :], kk[:, k, :], n, ALU.mult))
                link(dve.tensor_tensor(bb[:, k, :], kk[:, k, :], a_[:, k, :], ALU.mult))
                link(dve.tensor_scalar(a_[:, k, :], a_[:, k, :], 1.0, V[:, VA, k:k + 1], ALU.subtract, ALU.mult))
            for k in range(KD):
                link(dve.scalar_tensor_tensor(out=a_[:, k, :], in0=a_[:, k, :], scalar=1.0, in1=k_[:, k, :],
                                              op0=ALU.add, op1=ALU.mult))


def stage_recurrence(nc, K, S, O, y):
    H = 16
    HG = 4
    with Stage(nc, "scan") as s:
        r, logd, kk, bb, kf, v = (s.sb(x, [P, KD, P]) for x in ("r", "logd", "kk", "bb", "kf", "v"))
        L, before, after, minus = (s.sb(x, [P, KD, P]) for x in ("L", "exp_before", "exp_after", "exp_minus"))
        AR = s.sb("AR", [P, KD, 2, P])
        BF = s.sb("BF", [P, 2, KD, P])
        tok = s.sb("tok", [P, 3, KD, P])
        dend = s.sb("dend", [P, KD, 2])
        big = s.sb("big", [P, H, 2, 2, P])
        TT, Tm, om = s.sb("TT", [P, H, P]), s.sb("Tm", [P, H, P]), s.sb("om", [P, 2, H, P])
        X = before[:, :, :].rearrange("p k n -> p (k n)")
        X2 = minus[:, :, :].rearrange("p k n -> p (k n)")
        p1, sa = (t[:, :, :].rearrange("p k n -> p (k n)") for t in (L, after))
        Z = s.sb("Z", [P, KD, 2, DH])
        low = s.sb("low", [P, 2, P])
        level = s.sb("level", [P, NLV, P])
        U = [s.ps(f"u{i}", [P, 512]) for i in range(8)]
        (masks, ready, summed, exped, elem, turned, copied, made, masked, tt0, turned0, copied0, om_ready,
         x_made, x_copied, t_made, updated, p_made, p_copied, s_made, s_copied, z_made, z_done, y_made, y_copied, steps,
         pool_steps, w_turned, w_taken, stored) = (s.sem(x) for x in (
             "masks", "ready", "summed", "exped", "elem", "turned", "copied", "made", "masked", "tt0", "turned0",
             "copied0", "om_ready", "x_made", "x_copied", "t_made", "updated", "p_made", "p_copied", "s_made", "s_copied",
             "z_made", "z_done", "y_made", "y_copied", "steps", "pool_steps", "w_turned", "w_taken", "stored"))
        waited = s.sem("waited")
        block = s.block()

        def xs(g):
            return (X if g < 2 else X2)[:, (g % 2) * 512:(g % 2) * 512 + 512]

        def par(h):
            return slice((h % 2) * DH, (h % 2) * DH + DH)

        @block.sync
        def _(sp):
            with sp.Fori(0, NT) as i:
                sp.wait_ge(copied, 6 * i + 6)
                for dst, src in ((logd, S.logd), (kk, S.kk), (bb, S.bb), (kf, S.kf), (r, S.r), (v, S.v)):
                    sp.dma_start(dst[:, :, :], src[:, :, bass.ds(i * P, P)]).then_inc(ready, 16)
            sp.wait_ge(w_taken, 1)
            for a in range(2):
                sp.dma_start(O.wkv_p[0, 0].rearrange("(k a) i j -> a i k j", a=2)[a], L[par(a), :, 0:DH]).then_inc(stored, 16)
            sp.wait_ge(stored, 32)

        @block.gpsimd
        def _(pool):
            step = Link(pool, pool_steps)
            step(pool.memset(low[:], 1.0))
            step(pool.memset(level[:], 1.0))
            step(pool.memset(Z[:], 0.0))
            step(pool.affine_select(out=low[:, 0, :], in_=low[:, 0, :], compare_op=ALU.is_gt, fill=0.0, base=0,
                                    pattern=[[1, P]], channel_multiplier=-1))
            step(pool.affine_select(out=low[:, 1, :], in_=low[:, 1, :], compare_op=ALU.is_ge, fill=0.0, base=0,
                                    pattern=[[1, P]], channel_multiplier=-1))
            step(pool.memset(low[0:CHUNK, :, CHUNK:P], 0.0))
            for q in range(NLV):
                b = 1 << q
                v4 = level[:, q, :].rearrange("p (m h n) -> p m h n", h=2, n=b)
                step(pool.memset(v4[:, :, 0:1, :], 0.0))
                step(pool.affine_select(out=v4, in_=v4, compare_op=ALU.is_ge, fill=0.0, base=0,
                                        pattern=[[-2 * b, P // (2 * b)], [0, 2], [0, b]], channel_multiplier=1))
                step(pool.affine_select(out=v4, in_=v4, compare_op=ALU.is_gt, fill=0.0, base=b,
                                        pattern=[[2 * b, P // (2 * b)], [0, 2], [0, b]], channel_multiplier=-1))
            pool.sem_inc(masks, 1)
            with pool.Fori(0, NT) as i:
                for l in range(1, NLV):
                    if l == 1:
                        pool.wait_ge(masked, H * i + H)
                    if l >= 3:
                        pool.wait_ge(x_made, 20 * i + 4 * (l - 2))
                    pool.tensor_tensor(om[:, l % 2, :, :], big[:, :, 0, 0, :], level[:, l, :].unsqueeze(1).to_broadcast([P, H, P]),
                                       ALU.mult).then_inc(om_ready, 1)

        @block.tensor
        def _(pe):
            pe.wait_ge(masks, 1)
            with pe.Fori(0, NT) as i:
                pe.wait_ge(elem, i + 1)
                for n in range(6):
                    if n >= 2:
                        pe.wait_ge(copied, 6 * i + n + 5)
                    for f in range(4):
                        k = (n % 2) * 4 + f
                        src = BF[:, n // 2, k, :] if n < 4 else v[:, k, :]
                        last = pe.transpose(U[n % 2][:, f * P:(f + 1) * P], src, K.ident[:, :])
                    last.then_inc(turned, 1)
                for h in range(H):
                    if h >= 2:
                        pe.wait_ge(masked, H * i + h - 1)
                    for j in range(2):
                        last = pe.matmul(U[2 + h % 2][:, j * 256:(j + 1) * 256], BF[par(h), j, h // 2, :],
                                         AR[par(h), h // 2, :, :].rearrange("p a n -> p (a n)"), start=True, stop=True)
                    last.then_inc(made, 1)
                pe.wait_ge(tt0, i + 1)
                for g in range(4):
                    for u in range(HG):
                        last = pe.transpose(U[4 + g][:, u * P:(u + 1) * P], TT[:, g * HG + u, :], K.ident[:, :])
                    last.then_inc(turned0, 1)
                for l in range(1, NLV):
                    pe.wait_ge(om_ready, 5 * i + l)
                    for g in range(4):
                        if l == 1:
                            pe.wait_ge(copied0, 4 * i + g + 1)
                        else:
                            pe.wait_ge(updated, 36 * i + 8 * (l - 2) + 2 * g + 2)
                        if g >= 2:
                            pe.wait_ge(x_copied, 20 * i + 4 * (l - 1) + g - 1)
                        for u in range(HG):
                            h = g * HG + u
                            last = pe.matmul(U[g % 2][:, u * P:(u + 1) * P], om[:, l % 2, h, :], Tm[:, h, :], start=True, stop=True)
                        last.then_inc(x_made, 1)
                    for g in range(4):
                        pe.wait_ge(x_copied, 20 * i + 4 * (l - 1) + g + 1)
                        final = l == NLV - 1
                        if not final:
                            if g >= 2:
                                pe.wait_ge(updated, 36 * i + 8 * (l - 1) + 2 * (g - 2) + 2)
                            for u in range(HG):
                                last = pe.matmul(U[2 + g % 2][:, u * P:(u + 1) * P], TT[:, g * HG + u, :], xs(g)[:, u * P:(u + 1) * P],
                                                 start=True, stop=True)
                            last.then_inc(t_made, 1)
                        elif g >= 2:
                            pe.wait_ge(updated, 36 * i + 32 + g - 1)
                        for u in range(HG):
                            last = pe.matmul(U[4 + g % 2][:, u * P:(u + 1) * P], xs(g)[:, u * P:(u + 1) * P], TT[:, g * HG + u, :],
                                             start=True, stop=True)
                        last.then_inc(t_made, 1)
                pe.wait_ge(updated, 36 * i + 36)
                for c in range(2):
                    rows, cols = slice(c * CHUNK, (c + 1) * CHUNK), slice(c * CHUNK, (c + 1) * CHUNK)
                    ct = 2 * i + c
                    pe.wait_ge(z_done, ct + 1)
                    pe.wait_ge(y_copied, ct + 1)
                    pe.sem_inc(waited, 1)
                    for k in range(KD):
                        bank = U[k // 4][rows, k % 4 * P:(k % 4 + 1) * P]
                        pe.matmul(bank, AR[:, k, 0, cols], Z[:, k, :, :].rearrange("p a n -> p (a n)"), start=True, stop=False,
                                  skip_group_check=True)
                        for h in (2 * k, 2 * k + 1):
                            last = pe.matmul(bank[:, par(h)], big[:, h, 1, 0, cols], tok[:, 2, k, par(h)], start=False,
                                             stop=h % 2 == 1, skip_group_check=True)
                        if k % 4 == 3:
                            last.then_inc(p_made, 1)
                    for h in range(H):
                        if h % 8 == 0:
                            pe.wait_ge(p_copied, 2 * ct + h // 8 + 1)
                            pe.sem_inc(waited, 1)
                        last = pe.matmul(U[2 + h // 8][rows, h % 8 * DH:(h % 8 + 1) * DH], TT[:, h, cols],
                                         p1[:, h * DH:(h + 1) * DH], start=True, stop=True)
                        if h % 8 == 7:
                            last.then_inc(s_made, 1)
                    pe.wait_ge(s_copied, 2 * ct + 2)
                    pe.sem_inc(waited, 1)
                    for k in range(KD):
                        cs = slice(k * DH, (k + 1) * DH)
                        pe.matmul(U[5][:, cs], Z[:, k, :, :].rearrange("p a n -> p (a n)"), AR[:, k, 1, cols], start=True, stop=False,
                                  skip_group_check=True)
                        for h in (2 * k, 2 * k + 1):
                            dst = U[5][par(h), cs]
                            pe.matmul(dst, sa[:, h * DH:(h + 1) * DH], big[:, h, 0, 1, cols], start=False, stop=False, skip_group_check=True)
                            last = pe.matmul(dst, tok[:, 2, k, par(h)], big[:, h, 1, 1, cols], start=False, stop=True, skip_group_check=True)
                    last.then_inc(y_made, 1)
                    for h in range(H):
                        dst = U[4][par(h), h // 2 * DH:(h // 2 + 1) * DH]
                        pe.matmul(dst, tok[rows, 0, h // 2, par(h)], sa[rows, h * DH:(h + 1) * DH], start=True, stop=False)
                        last = pe.matmul(dst, tok[rows, 1, h // 2, par(h)], tok[rows, 2, h // 2, par(h)], start=False, stop=True)
                    last.then_inc(z_made, 1)
            pe.wait_ge(z_done, 2 * NT + 1)
            for k in range(KD):
                last = pe.transpose(U[k // 4][:, k % 4 * P:(k % 4 + 1) * P], Z[:, k, :, :].rearrange("p a n -> p (a n)"), K.ident[:, :])
            last.then_inc(w_turned, 1)

        @block.scalar
        def _(act):
            act.preload_act_table_set("natural_log_exp_and_others")
            act.sem_inc(y_copied, 1)
            act.sem_inc(copied, 6)
            with act.Fori(0, NT) as i:
                act.wait_ge(summed, i + 1)
                for dst, src, sign in ((before, before, 1.0), (after, L, 1.0), (minus, L, -1.0)):
                    act.activation(dst[:, :, :], src[:, :, :], ACT.Exp, scale=sign).then_inc(exped, 1)
                for n in range(6):
                    act.wait_ge(turned, 6 * i + n + 1)
                    act.activation(tok[:, n // 2, (n % 2) * 4:(n % 2) * 4 + 4, :], U[n % 2][:, :].rearrange("p (k n) -> p k n", k=4),
                                   ACT.Copy).then_inc(copied, 1)
                for g in range(4):
                    act.wait_ge(turned0, 4 * i + g + 1)
                    act.activation(Tm[:, g * HG:(g + 1) * HG, :], U[4 + g][:, :].rearrange("p (k n) -> p k n", k=4), ACT.Copy)\
                       .then_inc(copied0, 1)
                for l in range(1, NLV):
                    for g in range(4):
                        act.wait_ge(x_made, 20 * i + 4 * (l - 1) + g + 1)
                        act.activation(xs(g), U[g % 2][:, :], ACT.Copy).then_inc(x_copied, 1)
                for c in range(2):
                    rows = slice(c * CHUNK, (c + 1) * CHUNK)
                    ct = 2 * i + c
                    for q in range(2):
                        act.wait_ge(p_made, 2 * ct + q + 1)
                        act.activation(p1[rows, q * 512:(q + 1) * 512], U[q][rows, :], ACT.Copy).then_inc(p_copied, 1)
                    for q in range(2):
                        act.wait_ge(s_made, 2 * ct + q + 1)
                        act.activation(sa[rows, q * 512:(q + 1) * 512], U[2 + q][rows, :], ACT.Copy).then_inc(s_copied, 1)
                    act.wait_ge(y_made, ct + 1)
                    act.activation(y[:, :, bass.ds(i * P + c * CHUNK, CHUNK)], U[5][:, :].rearrange("p (k n) -> p k n", k=KD), ACT.Copy)\
                       .then_inc(y_copied, 1)
            act.wait_ge(w_turned, 1)
            for q in range(2):
                for a in range(2):
                    last = act.activation(L[par(a), q * 4:q * 4 + 4, 0:DH],
                                          U[q][par(a), :].rearrange("p (k n) -> p k n", k=4)[:, :, par(a)], ACT.Copy)
            last.then_inc(w_taken, 1)

        @block.vector
        def _(dve):
            dve.wait_ge(masks, 1)
            dve.sem_inc(z_done, 1)
            link = Link(dve, steps)
            per = 10
            with dve.Fori(0, NT) as i:
                link.enter(i, per)
                dve.wait_ge(ready, 96 * (i + 1))
                for k in range(KD):
                    for c in range(2):
                        ts = slice(c * CHUNK, (c + 1) * CHUNK)
                        last = dve.tensor_tensor_scan(L[:, k, ts], K.ones[:, 0:CHUNK], logd[:, k, ts], 0.0, ALU.mult, ALU.add)
                link(last)
                dve.tensor_tensor(before[:, :, :], L[:, :, :], logd[:, :, :], ALU.subtract).then_inc(summed, 1)
                dve.wait_ge(exped, 3 * i + 3)
                dve.scalar_tensor_tensor(out=AR[:, :, 0, :], in0=kk[:, :, :], scalar=-1.0, in1=before[:, :, :], op0=ALU.mult, op1=ALU.mult)
                dve.tensor_tensor(AR[:, :, 1, :], r[:, :, :], after[:, :, :], ALU.mult)
                for c in range(2):
                    dve.tensor_copy(dend[:, :, c:c + 1], after[:, :, c * CHUNK + CHUNK - 1:c * CHUNK + CHUNK])
                dve.tensor_tensor(BF[:, 0, :, :], bb[:, :, :], minus[:, :, :], ALU.mult)
                dve.tensor_tensor(BF[:, 1, :, :], kf[:, :, :], minus[:, :, :], ALU.mult).then_inc(elem, 1)
                for h in range(H):
                    dve.wait_ge(made, H * i + h + 1)
                    dve.tensor_tensor(big[:, h].rearrange("p b a n -> p b (a n)"), U[2 + h % 2][:, :].rearrange("p (b m) -> p b m", b=2),
                                      low[:, :, :].rearrange("p a n -> p (a n)").unsqueeze(1).to_broadcast([P, 2, 2 * P]),
                                      ALU.mult).then_inc(masked, 1)
                dve.wait_ge(masked, H * i + H)
                link(dve.tensor_tensor(TT[:, :, :], big[:, :, 0, 0, :], level[:, 0, :].unsqueeze(1).to_broadcast([P, H, P]), ALU.mult))
                dve.tensor_tensor(TT[:, :, :], TT[:, :, :], K.ident[:, :].unsqueeze(1).to_broadcast([P, H, P]), ALU.add).then_inc(tt0, 1)
                for l in range(1, NLV):
                    final = l == NLV - 1
                    for g in range(4):
                        gs = slice(g * HG, (g + 1) * HG)
                        for q in range(1 if final else 2):
                            dve.wait_ge(t_made, 36 * i + (32 + g + 1 if final else 8 * (l - 1) + 2 * g + q + 1))
                            dst, bank = (TT, 4) if final or q == 1 else (Tm, 2)
                            if q == 0:
                                if not final:
                                    dve.wait_ge(t_made, 36 * i + 8 * (l - 1) + 2 * g + 2)
                            dve.tensor_tensor(dst[:, gs, :], dst[:, gs, :], U[bank + g % 2][:, :].rearrange("p (k n) -> p k n", k=HG),
                                              ALU.add).then_inc(updated, 1)
                for c in range(2):
                    ct = 2 * i + c
                    dve.wait_ge(z_made, ct + 1)
                    for a in range(2):
                        za, n = Z[par(a), :, a, :], U[4][par(a), :].rearrange("p (k n) -> p k n", k=KD)
                        link(dve.tensor_tensor(za, za, n, ALU.add))
                        link(dve.tensor_tensor(za, za, dend[par(a), :, c:c + 1].to_broadcast([DH, KD, DH]), ALU.mult))
                    dve.sem_inc(z_done, 1)
            link.leave(NT, per)


def stage_recurrence_sample(nc, K, I, S, O, yrow):
    with Stage(nc, "sscan") as s:
        st = s.sb("state", [P, DH, DH])
        tmp = s.sb("tmp", [P, DH, DH])
        names = ("r", "logd", "kk", "bb", "kf", "v")
        inp = {n: s.sb(n, [P, NQ, DH]) for n in names}
        sa, ys = s.sb("sa", [P, DH]), s.sb("ys", [P, NQ, DH])
        loaded, exped, steps, stored = s.sem("loaded"), s.sem("exped"), s.sem("steps"), s.sem("stored")
        block = s.block()

        @block.sync
        def _(sp):
            sp.dma_start(st[:, :, :], I.state_wkv[0].rearrange("b h i j -> (b h) i j")).then_inc(loaded, 16)
            for n in names:
                src = S.new[n].rearrange("(b q) (h j) -> b h q j", b=NB, h=16)
                for b in range(NB):
                    sp.dma_start(inp[n][b * 16:(b + 1) * 16, :, :], src[b]).then_inc(loaded, 16)
            sp.wait_ge(steps, 9 * NQ)
            sp.dma_start(O.wkv_s[0].rearrange("b h i j -> (b h) i j"), st[:, :, :]).then_inc(stored, 16)
            dst = yrow.rearrange("(b q) (h j) -> b h q j", b=NB, h=16)
            for b in range(NB):
                sp.dma_start(dst[b], ys[b * 16:(b + 1) * 16, :, :]).then_inc(stored, 16)
            sp.wait_ge(stored, 16 * (NB + 1))

        @block.scalar
        def _(act):
            act.wait_ge(loaded, 16 * (1 + 6 * NB))
            act.activation(inp["logd"][:, :, :], inp["logd"][:, :, :], ACT.Exp).then_inc(exped, 1)

        @block.vector
        def _(dve):
            link = Link(dve, steps)
            dve.wait_ge(loaded, 16 * (1 + 6 * NB))
            dve.wait_ge(exped, 1)
            full = [P, DH, DH]

            def over_i(t, q):
                return t[:, q, :].unsqueeze(1).to_broadcast(full)

            for q in range(NQ):
                link(dve.tensor_tensor(tmp[:, :, :], st[:, :, :], over_i(inp["kk"], q), ALU.mult))
                link(dve.tensor_reduce(sa[:, :], tmp[:, :, :], AX.X, ALU.add))
                link(dve.tensor_tensor(st[:, :, :], st[:, :, :], over_i(inp["logd"], q), ALU.mult))
                link(dve.tensor_tensor(tmp[:, :, :], sa[:, :].unsqueeze(2).to_broadcast(full), over_i(inp["bb"], q), ALU.mult))
                link(dve.tensor_tensor(st[:, :, :], st[:, :, :], tmp[:, :, :], ALU.subtract))
                link(dve.tensor_tensor(tmp[:, :, :], inp["v"][:, q, :].unsqueeze(2).to_broadcast(full), over_i(inp["kf"], q), ALU.mult))
                link(dve.tensor_tensor(st[:, :, :], st[:, :, :], tmp[:, :, :], ALU.add))
                link(dve.tensor_tensor(tmp[:, :, :], st[:, :, :], over_i(inp["r"], q), ALU.mult))
                link(dve.tensor_reduce(ys[:, q, :], tmp[:, :, :], AX.X, ALU.add))


def stage_sample_rows(nc, K, yrow, y):
    with Stage(nc, "srows") as s:
        rows = s.sb("rows", [NS, D])
        tp = s.ps("tp", [P, KD, NS])
        loaded, turned, taken = s.sem("loaded"), s.sem("turned"), s.sem("taken")
        block = s.block()

        @block.sync
        def _(sp):
            sp.dma_start(rows[:, :], yrow).then_inc(loaded, 16)

        @block.tensor
        def _(pe):
            pe.wait_ge(loaded, 16)
            for k in range(KD):
                last = pe.transpose(tp[:, k, :], rows[:, k * P:(k + 1) * P], K.ident[0:NS, 0:NS])
            last.then_inc(turned, 1)

        @block.vector
        def _(dve):
            dve.wait_ge(turned, 1)
            dve.tensor_copy(y[:, :, SEQ:T], tp[:, :, :]).then_inc(taken, 1)


def stage_rwkv_out(nc, K, S, V, y):
    VR, VW, VB = (VECTORS.index(x) for x in ("r_k", "ln_w", "ln_b"))
    with Stage(nc, "gn") as s:
        ins = [s.sb(f"ins{i}", [P, 4, T]) for i in range(2)]
        sq, rstd, rk = s.sb("sq", [P, T]), s.sb("rstd", [P, T]), s.sb("rk", [P, T])
        eps = s.sb("eps", [P, 1])
        halves = s.sb("halves", [P, P])
        total = [s.ps(f"total{i}", [P, NCH, 512]) for i in range(2)]
        steps, product, rooted, filled, used = s.sem("steps"), s.sem("product"), s.sem("rooted"), s.sem("filled"), s.sem("used")
        loaded = [s.sem(f"loaded{i}") for i in range(2)]
        asked = s.sem("asked")
        block = s.block()

        @block.gpsimd
        def _(pool):
            fill_halves(pool, halves, filled)
            pool.wait_ge(filled, 3)
            pool.memset(eps[:, :], 64e-5).then_inc(filled, 1)

        @block.sync
        def _(sp):
            for k in range(KD):
                if k >= 2:
                    sp.wait_ge(used, k - 1)
                for j, src in enumerate((S.r, S.kf, S.v, S.g)):
                    sp.dma_start(ins[k % 2][:, j, :], src[:, k, :]).then_inc(loaded[k % 2], 16)

        @block.tensor
        def _(pe):
            pe.wait_ge(filled, 3)
            for n in range(3 * KD):
                k, j = n // 3, n % 3
                pe.wait_ge(asked, n + 1)
                src = (y[:, k, :], sq[:, :], rk[:, :])[j]
                bank = total[0] if j == 0 else total[1] if j == 1 else total[0]
                for c in range(NCH):
                    last = pe.matmul(bank[:, c, 0:CW], halves[:, :], src[:, c * CW:(c + 1) * CW], start=True, stop=True)
                last.then_inc(product, 1)

        @block.scalar
        def _(act):
            act.wait_ge(filled, 4)
            for k in range(KD):
                act.wait_ge(product, 3 * k + 2)
                act.activation(row3(rstd[:, :]), chunks(total[1]), ACT.Sqrt, bias=eps[:, 0:1], scale=1.0 / DH).then_inc(rooted, 1)

        @block.vector
        def _(dve):
            link = Link(dve, steps)
            for k in range(KD):
                i4 = ins[k % 2]
                yk = y[:, k, :]
                dve.sem_inc(asked, 1)
                dve.wait_ge(product, 3 * k + 1)
                link(dve.scalar_tensor_tensor(out=row3(yk), in0=chunks(total[0]), scalar=-1.0 / DH, in1=row3(yk), op0=ALU.mult, op1=ALU.add))
                link(dve.tensor_tensor(sq[:, :], yk, yk, ALU.mult))
                dve.sem_inc(asked, 1)
                dve.wait_ge(loaded[k % 2], 64 * (k // 2 + 1))
                link(dve.scalar_tensor_tensor(out=rk[:, :], in0=i4[:, 0, :], scalar=V[:, VR, k:k + 1], in1=i4[:, 1, :],
                                              op0=ALU.mult, op1=ALU.mult))
                dve.sem_inc(asked, 1)
                dve.wait_ge(rooted, k + 1)
                link(dve.reciprocal(rstd[:, :], rstd[:, :]))
                link(dve.scalar_tensor_tensor(out=yk, in0=yk, scalar=V[:, VW, k:k + 1], in1=rstd[:, :], op0=ALU.mult, op1=ALU.mult))
                dve.wait_ge(product, 3 * k + 3)
                link(dve.tensor_tensor(row3(i4[:, 2, :]), chunks(total[0]), row3(i4[:, 2, :]), ALU.mult))
                link(dve.scalar_tensor_tensor(out=yk, in0=yk, scalar=V[:, VB, k:k + 1], in1=i4[:, 2, :], op0=ALU.add, op1=ALU.add))
                link(dve.tensor_tensor(yk, yk, i4[:, 3, :], ALU.mult))
                dve.sem_inc(used, 1)


def rwkv(nc, K, I, O, x, h):
    S = Names()
    S.r, S.logd, S.kk, S.bb, S.kf, S.v, S.g = (
        nc.dram_tensor(f"s_{n}", (P, KD, T), F32).ap() for n in ("r", "logd", "kk", "bb", "kf", "v", "g"))
    S.new = {n: nc.dram_tensor(f"s_{n}_new", (NS, D), F32).ap() for n in ("r", "logd", "kk", "bb", "kf", "v")}
    yrow = nc.dram_tensor("s_y_new", (NS, D), F32).ap()
    with ExitStack() as outer:
        V = outer.enter_context(nc.sbuf_tensor("vectors", [P, len(VECTORS), KD], F32))
        stage_norm(nc, K, "rpre", x, I.norm_mix_pre[1], h)
        with ExitStack() as c:
            prev = c.enter_context(nc.sbuf_tensor("prev", [P, KD, NB], F32))
            stage_rwkv_vectors(nc, K, I, h, V, prev, O)
            xx, m, z = (c.enter_context(nc.sbuf_tensor(n, [P, KD, T], F32)) for n in ("xx", "mixed", "projected"))
            stage_shift(nc, K, h, prev, xx)
            stage_mix(nc, K, 0, h, xx, V, m)
            stage_linear(nc, K, "rr", m, KD, column_loads(I.rk_w_r[0], KD), KD, z)
            stage_keep(nc, K, "keepr", z, S.r, S.new["r"])
            stage_mix(nc, K, 3, h, xx, V, m)
            stage_linear(nc, K, "rv", m, KD, column_loads(I.rk_w_v[0], KD), KD, z)
            stage_keep(nc, K, "keepv", z, S.v, S.new["v"])
            stage_mix(nc, K, 1, h, xx, V, m)
            stage_lora(nc, K, "lw", m, I.rk_w1[0], I.rk_w2[0], 64, ACT.Tanh, V[:, VECTORS.index("w0"), :], ACT.Sigmoid, z)
            stage_keep(nc, K, "keepw", z, S.logd, S.new["logd"], scale=DECAY)
            stage_mix(nc, K, 5, h, xx, V, m)
            stage_lora(nc, K, "lg", m, I.rk_g1[0], I.rk_g2[0], 160, ACT.Sigmoid, None, ACT.Copy, z)
            stage_keep(nc, K, "keepg", z, S.g, None)
            stage_mix(nc, K, 4, h, xx, V, m)
            stage_lora(nc, K, "la", m, I.rk_a1[0], I.rk_a2[0], 64, ACT.Copy, V[:, VECTORS.index("a0"), :], ACT.Sigmoid, z)
            stage_mix(nc, K, 2, h, xx, V, m)
            stage_linear(nc, K, "rk", m, KD, column_loads(I.rk_w_k[0], KD), KD, xx)
            stage_keys(nc, K, V, xx, z, h, m)
            stage_keep(nc, K, "keepkk", h, S.kk, S.new["kk"])
            stage_keep(nc, K, "keepbb", m, S.bb, S.new["bb"])
            stage_keep(nc, K, "keepkf", z, S.kf, S.new["kf"])
        stage_recurrence(nc, K, S, O, h)
        stage_recurrence_sample(nc, K, I, S, O, yrow)
        stage_sample_rows(nc, K, yrow, h)
        stage_rwkv_out(nc, K, S, V, h)
        with ExitStack() as c:
            z = c.enter_context(nc.sbuf_tensor("mixer_out", [P, KD, T], F32))
            stage_linear(nc, K, "ro", h, KD, column_loads(I.rk_w_o[0], KD), KD, z)
            stage_norm(nc, K, "rpost", z, I.norm_mix_post[1], z, residual=x, square=h)


class Names:
    pass


def build(nc, I, O, K):
    ctx = ExitStack()

    def sb(c, name, shape, dt=F32):
        return c.enter_context(nc.sbuf_tensor(name, shape, dt))

    with ctx:
        K.ones, K.ident = sb(ctx, "ones", [P, P]), sb(ctx, "ident", [P, P])
        K.eps = sb(ctx, "eps", [P, 1])
        K.x_save = nc.dram_tensor("x_save", (P, KD, T), F32).ap()
        oT = sb(ctx, "oT", [P, KD, T])
        with ExitStack() as att:
            K.negones, K.tri, K.before, K.bound, K.causal = (
                sb(att, n, [P, P]) for n in ("negones", "tri", "before", "bound", "causal"))
            K.one = sb(att, "one", [P, 1])
            K.zeros16 = sb(att, "zeros16", [P, 512], BF16)
            stage_constants(nc, K)
            stage_load_x(nc, K, I.x_prompt, I.x_sample, oT)
            A = Names()
            A.qa, A.ka, A.qb, A.qi = (sb(att, n, [P, HP, T]) for n in ("qa", "ka", "qb", "qi"))
            A.kb, A.ki = (sb(att, n, [P, 1, T]) for n in ("kb", "ki"))
            A.same = sb(att, "same", [NS, NS])
            A.wtok = sb(att, "wtok", [P, NT + 1, 8])
            A.vtok = sb(att, "vtok", [P, NT, 640])
            with ExitStack() as c:
                A.va, A.vb, A.wi = sb(c, "va", [P, HP, T]), sb(c, "vb", [P, 1, T]), sb(c, "wi", [8, T])
                with ExitStack() as c2:
                    hT = sb(c2, "hT", [P, KD, T])
                    stage_norm(nc, K, "norm0", oT, I.norm_mix_pre[0], hT)
                    stage_project(nc, K, I.att_w_in, hT, A, oT)
                stage_rows(nc, K, A, O)
            stage_stick_prompt(nc, K, A, oT)
            stage_sparse_prompt(nc, K, A, oT)
            A.score = A.vtok[0:NS, :, :].rearrange("p t n -> p (t n)")
            stage_index_sample(nc, K, A, I)
            stage_stick_sample(nc, K, A, I, O, oT)
            stage_sparse_sample(nc, K, A, I, O, oT)
        h = sb(ctx, "h", [P, KD, T])
        stage_linear(nc, K, "aout", oT, KD, attention_out_loads(I.att_w_out[0]), KD, h)
        x = oT
        stage_reload(nc, "reload", K.x_save, x)
        stage_norm(nc, K, "apost", h, I.norm_mix_post[0], h, residual=x)
        ffn(nc, K, I, O, 0, x, h)
        rwkv(nc, K, I, O, x, h)
        ffn(nc, K, I, O, 1, x, h)
        stage_y(nc, K, "y", x, O.y_prompt, O.y_sample)


NAMES = ['x_prompt', 'x_sample', 'cache_sb_k', 'cache_sb_v', 'cache_dsa_k', 'cache_dsa_v', 'cache_idx_k', 'page_table',
         'state_wkv', 'state_shift', 'state_ffn_conv', 'norm_mix_pre', 'norm_mix_post', 'norm_ffn_pre', 'norm_ffn_post',
         'att_w_in', 'att_w_out', 'rk_mix', 'rk_w_r', 'rk_w_k', 'rk_w_v', 'rk_w_o', 'rk_w0', 'rk_w1', 'rk_w2',
         'rk_a0', 'rk_a1', 'rk_a2', 'rk_g1', 'rk_g2', 'rk_k_k', 'rk_k_a', 'rk_r_k', 'rk_ln_w', 'rk_ln_b',
         'ffn_w_up', 'ffn_conv_w', 'ffn_conv_b', 'ffn_w_down']
OUTS = [('y_prompt', (1, SEQ, D)), ('y_sample', (NB, NQ, D)),
        ('sb_k_p', (1, 1, SEQ, 8, DH)), ('sb_k_s', (1, NB, NQ, 8, DH)), ('sb_v_p', (1, 1, SEQ, 8, DH)), ('sb_v_s', (1, NB, NQ, 8, DH)),
        ('dsa_k_p', (1, 1, SEQ, 2, DH)), ('dsa_k_s', (1, NB, NQ, 2, DH)), ('dsa_v_p', (1, 1, SEQ, 2, DH)), ('dsa_v_s', (1, NB, NQ, 2, DH)),
        ('idx_k_p', (1, 1, SEQ, DH)), ('idx_k_s', (1, NB, NQ, DH)),
        ('wkv_p', (1, 1, 16, DH, DH)), ('wkv_s', (1, NB, 16, DH, DH)), ('shift_p', (1, 1, D)), ('shift_s', (1, NB, D)),
        ('ffn_conv_p', (2, 1, 2, 2 * D_FF)), ('ffn_conv_s', (2, NB, 2, 2 * D_FF))]


def kernel(x_prompt, x_sample, cache_sb_k, cache_sb_v, cache_dsa_k, cache_dsa_v, cache_idx_k, page_table,
           state_wkv, state_shift, state_ffn_conv, norm_mix_pre, norm_mix_post, norm_ffn_pre, norm_ffn_post,
           att_w_in, att_w_out, rk_mix, rk_w_r, rk_w_k, rk_w_v, rk_w_o, rk_w0, rk_w1, rk_w2, rk_a0, rk_a1, rk_a2,
           rk_g1, rk_g2, rk_k_k, rk_k_a, rk_r_k, rk_ln_w, rk_ln_b, ffn_w_up, ffn_conv_w, ffn_conv_b, ffn_w_down):
    import numpy as np
    import concourse.bacc as bacc
    from concourse.bass_utils import run_bass_kernel_spmd as run

    nc = bacc.Bacc("TRN2", target_bir_lowering=False, num_devices=1)
    given = dict(zip(NAMES, (
        x_prompt, x_sample, cache_sb_k, cache_sb_v, cache_dsa_k, cache_dsa_v, cache_idx_k, page_table,
        state_wkv, state_shift, state_ffn_conv, norm_mix_pre, norm_mix_post, norm_ffn_pre, norm_ffn_post,
        att_w_in, att_w_out, rk_mix, rk_w_r, rk_w_k, rk_w_v, rk_w_o, rk_w0, rk_w1, rk_w2, rk_a0, rk_a1, rk_a2,
        rk_g1, rk_g2, rk_k_k, rk_k_a, rk_r_k, rk_ln_w, rk_ln_b, ffn_w_up, ffn_conv_w, ffn_conv_b, ffn_w_down)))
    pos = np.concatenate([np.arange(SEQ), np.tile(PAST + np.arange(NQ), NB)]).astype(np.float32)
    inv = (10000.0 ** (-2.0 * np.arange(DH // 2) / DH)).astype(np.float32)
    ang = (pos[None, :] * inv[:, None]).astype(np.float32)
    given["rope_cos"] = np.ascontiguousarray(np.tile(np.cos(ang), (4, 1)).astype(np.float32))
    given["rope_sin"] = np.ascontiguousarray(np.concatenate([np.sin(ang), -np.sin(ang)] * 2, 0).astype(np.float32))
    arrays, aps = {}, {}
    for name, a in given.items():
        a = np.ascontiguousarray(a)
        arrays[f"in_{name}"] = a
        aps[name] = nc.dram_tensor(f"in_{name}", a.shape, mybir.dt.from_np(a.dtype), kind="ExternalInput").ap()
    outs = {n: nc.dram_tensor(f"out_{n}", shape, F32, kind="ExternalOutput").ap() for n, shape in OUTS}
    I, O, K = Names(), Names(), Names()
    (I.x_prompt, I.x_sample, I.cache_sb_k, I.cache_sb_v, I.cache_dsa_k, I.cache_dsa_v, I.cache_idx_k,
     I.page_table, I.state_wkv, I.state_shift, I.state_ffn_conv, I.norm_mix_pre, I.norm_mix_post,
     I.norm_ffn_pre, I.norm_ffn_post, I.att_w_in, I.att_w_out, I.rk_mix, I.rk_w_r, I.rk_w_k, I.rk_w_v,
     I.rk_w_o, I.rk_w0, I.rk_w1, I.rk_w2, I.rk_a0, I.rk_a1, I.rk_a2, I.rk_g1, I.rk_g2, I.rk_k_k, I.rk_k_a,
     I.rk_r_k, I.rk_ln_w, I.rk_ln_b, I.ffn_w_up, I.ffn_conv_w, I.ffn_conv_b, I.ffn_w_down) = (aps[n] for n in NAMES)
    (O.y_prompt, O.y_sample, O.sb_k_p, O.sb_k_s, O.sb_v_p, O.sb_v_s, O.dsa_k_p, O.dsa_k_s, O.dsa_v_p,
     O.dsa_v_s, O.idx_k_p, O.idx_k_s, O.wkv_p, O.wkv_s, O.shift_p, O.shift_s, O.ffn_conv_p, O.ffn_conv_s) = (outs[n] for n, _ in OUTS)
    K.cos, K.sin = aps["rope_cos"], aps["rope_sin"]
    build(nc, I, O, K)
    r = run(nc, [arrays], core_ids=[0])
    return tuple(r.results[0][f"out_{n}"] for n, _ in OUTS)
```
